# Optimizing a Trainium2 kernel written in Bass

```python
import math
import jax, jax.numpy as jnp
from jax import lax
import numpy as np

D_MODEL = 2048
BATCH = 1
SEQ = 256
DEPTH = 1

HEAD_DIM = 128
ROPE_FRAC_DIV = 4
ROPE_DIM = HEAD_DIM // ROPE_FRAC_DIV
ROPE_THETA = 500000.0
DSA_HEADS = 8
DSA_W = DSA_HEADS * HEAD_DIM
DSA_Q_RANK = 512
IDX_HEADS = 16
IDX_DIM = 64
IDX_ROPE_DIM = IDX_DIM // ROPE_FRAC_DIV
IDX_TOPK = 256
IDX_Q_BLOCK = 128
MOBA_HEADS = 8
MOBA_W = MOBA_HEADS * HEAD_DIM
MOBA_BLOCK = 256
MOBA_TOPK = 3
MOBA_Q_BLOCK = 32
MEM_LEN = 256
MEM_HEADS = 4
MEM_HEAD_DIM = 128
MEM_W = MEM_HEADS * MEM_HEAD_DIM
D_FF = 4 * D_MODEL
EPS = 1e-6
IN_SIZES = (DSA_Q_RANK, DSA_W, DSA_W, IDX_DIM, IDX_HEADS, MOBA_W, MOBA_W, MOBA_W, D_MODEL, D_MODEL)
IN_COLS = DSA_Q_RANK + 2 * DSA_W + IDX_DIM + IDX_HEADS + 3 * MOBA_W + 2 * D_MODEL


def _split_points():
    pts, acc = [], 0
    for s in IN_SIZES[:-1]:
        acc += s
        pts.append(acc)
    return pts

def rmsnorm(x, g):
    x32 = x.astype(jnp.float32)
    y = x32 * lax.rsqrt(jnp.mean(x32 * x32, axis=-1, keepdims=True) + EPS)
    return (y * g.astype(jnp.float32)).astype(x.dtype)

def rope_partial(x, pos, rot_dim):
    half = rot_dim // 2
    inv = ROPE_THETA ** (-jnp.arange(half, dtype=jnp.float32) * (2.0 / rot_dim))
    ang = pos.astype(jnp.float32)[..., None] * inv
    cos = jnp.cos(ang)[:, :, None, :]
    sin = jnp.sin(ang)[:, :, None, :]
    xr = x[..., :rot_dim].astype(jnp.float32)
    x1, x2 = xr[..., :half], xr[..., half:]
    rot = jnp.concatenate([x1 * cos - x2 * sin, x2 * cos + x1 * sin], axis=-1).astype(x.dtype)
    return jnp.concatenate([rot, x[..., rot_dim:]], axis=-1)

def dsa_branch(c_q, k, v, k_idx, w_idx, g_cq, w_uq, w_iq, pos):
    B, S, _ = k.shape
    c_q = rmsnorm(c_q, g_cq)
    q = rope_partial((c_q @ w_uq).reshape(B, S, DSA_HEADS, HEAD_DIM), pos, ROPE_DIM)
    q_idx = rope_partial((c_q @ w_iq).reshape(B, S, IDX_HEADS, IDX_DIM), pos, IDX_ROPE_DIM)
    k = rope_partial(k.reshape(B, S, DSA_HEADS, HEAD_DIM), pos, ROPE_DIM)
    v = v.reshape(B, S, DSA_HEADS, HEAD_DIM)
    k_idx = rope_partial(k_idx[:, :, None, :], pos, IDX_ROPE_DIM)[:, :, 0, :]
    w_idx = w_idx.astype(jnp.float32) * (IDX_HEADS ** -0.5 * IDX_DIM ** -0.5)
    n_sel = min(IDX_TOPK, S // 4)
    n_blocks = S // IDX_Q_BLOCK
    key_pos = jnp.arange(S)
    scale = HEAD_DIM ** -0.5

    def block(i):
        start = i * IDX_Q_BLOCK
        qb = lax.dynamic_slice_in_dim(q, start, IDX_Q_BLOCK, axis=1)
        qib = lax.dynamic_slice_in_dim(q_idx, start, IDX_Q_BLOCK, axis=1)
        wb = lax.dynamic_slice_in_dim(w_idx, start, IDX_Q_BLOCK, axis=1)
        t = start + jnp.arange(IDX_Q_BLOCK)
        logits = jnp.einsum('bqhd,bsd->bqhs', qib, k_idx).astype(jnp.float32)
        score = jnp.einsum('bqh,bqhs->bqs', wb, jax.nn.relu(logits))
        causal = key_pos[None, :] <= t[:, None]
        score = jnp.where(causal[None], score, -jnp.inf)
        _, sel = lax.top_k(score, n_sel)
        valid = sel <= t[None, :, None]
        kg = jax.vmap(lambda kk, ii: kk[ii])(k, sel)
        vg = jax.vmap(lambda vv, ii: vv[ii])(v, sel)
        s = jnp.einsum('bqhd,bqnhd->bhqn', qb, kg).astype(jnp.float32) * scale
        s = jnp.where(valid[:, None], s, -jnp.inf)
        p = jax.nn.softmax(s, axis=-1).astype(v.dtype)
        o = jnp.einsum('bhqn,bqnhd->bqhd', p, vg)
        return o.reshape(B, IDX_Q_BLOCK, DSA_W)

    out = lax.map(block, jnp.arange(n_blocks))
    return out.transpose(1, 0, 2, 3).reshape(B, S, DSA_W)

def moba_branch(q, k, v, pos):
    B, S, _ = q.shape
    q = rope_partial(q.reshape(B, S, MOBA_HEADS, HEAD_DIM), pos, ROPE_DIM)
    k = rope_partial(k.reshape(B, S, MOBA_HEADS, HEAD_DIM), pos, ROPE_DIM)
    v = v.reshape(B, S, MOBA_HEADS, HEAD_DIM)
    nb = -(-S // MOBA_BLOCK)
    pad = nb * MOBA_BLOCK - S
    kp = jnp.pad(k, ((0, 0), (0, pad), (0, 0), (0, 0)))
    vp = jnp.pad(v, ((0, 0), (0, pad), (0, 0), (0, 0)))
    kblk = kp.reshape(B, nb, MOBA_BLOCK, MOBA_HEADS, HEAD_DIM)
    vblk = vp.reshape(B, nb, MOBA_BLOCK, MOBA_HEADS, HEAD_DIM)
    kmean = jnp.mean(kblk.astype(jnp.float32), axis=2).astype(k.dtype)
    kbh = kblk.transpose(0, 3, 1, 2, 4)
    vbh = vblk.transpose(0, 3, 1, 2, 4)
    n_sel = min(MOBA_TOPK, nb - 1)
    n_qblocks = S // MOBA_Q_BLOCK
    scale = HEAD_DIM ** -0.5
    gather2 = jax.vmap(jax.vmap(lambda kk, ii: kk[ii]))

    def block(i):
        start = i * MOBA_Q_BLOCK
        qb = lax.dynamic_slice_in_dim(q, start, MOBA_Q_BLOCK, axis=1)
        t = start + jnp.arange(MOBA_Q_BLOCK)
        cur = start // MOBA_BLOCK
        own_k = lax.dynamic_slice_in_dim(kp, cur * MOBA_BLOCK, MOBA_BLOCK, axis=1)
        own_v = lax.dynamic_slice_in_dim(vp, cur * MOBA_BLOCK, MOBA_BLOCK, axis=1)
        own_pos = cur * MOBA_BLOCK + jnp.arange(MOBA_BLOCK)
        s_own = jnp.einsum('bqhd,bkhd->bhqk', qb, own_k).astype(jnp.float32) * scale
        s_own = jnp.where((own_pos[None, :] <= t[:, None])[None, None], s_own, -jnp.inf)
        if n_sel > 0:
            gate = jnp.einsum('bqhd,bnhd->bhqn', qb, kmean).astype(jnp.float32)
            gate = jnp.where(jnp.arange(nb) < cur, gate, -jnp.inf)
            _, sel = lax.top_k(gate, n_sel)
            valid = sel < cur
            kg = gather2(kbh, sel)
            vg = gather2(vbh, sel)
            qbh = qb.transpose(0, 2, 1, 3)
            s_sel = jnp.einsum('bhqd,bhqnkd->bhqnk', qbh, kg).astype(jnp.float32) * scale
            s_sel = jnp.where(valid[..., None], s_sel, -jnp.inf)
            s_sel = s_sel.reshape(B, MOBA_HEADS, MOBA_Q_BLOCK, n_sel * MOBA_BLOCK)
            p = jax.nn.softmax(jnp.concatenate([s_sel, s_own], axis=-1), axis=-1).astype(v.dtype)
            p_sel = p[..., :n_sel * MOBA_BLOCK].reshape(B, MOBA_HEADS, MOBA_Q_BLOCK, n_sel, MOBA_BLOCK)
            p_own = p[..., n_sel * MOBA_BLOCK:]
            o = (jnp.einsum('bhqnk,bhqnkd->bqhd', p_sel, vg)
                 + jnp.einsum('bhqk,bkhd->bqhd', p_own, own_v))
        else:
            p_own = jax.nn.softmax(s_own, axis=-1).astype(v.dtype)
            o = jnp.einsum('bhqk,bkhd->bqhd', p_own, own_v)
        return o.reshape(B, MOBA_Q_BLOCK, MOBA_W)

    out = lax.map(block, jnp.arange(n_qblocks))
    return out.transpose(1, 0, 2, 3).reshape(B, S, MOBA_W)

def mem_cross_attn(h, mem_n, w_q, w_kv, w_o):
    B, S, _ = h.shape
    M = mem_n.shape[1]
    q = (h @ w_q).reshape(B, S, MEM_HEADS, MEM_HEAD_DIM)
    kv = mem_n @ w_kv
    k = kv[..., :MEM_W].reshape(B, M, MEM_HEADS, MEM_HEAD_DIM)
    v = kv[..., MEM_W:].reshape(B, M, MEM_HEADS, MEM_HEAD_DIM)
    s = jnp.einsum('bshd,bmhd->bhsm', q, k).astype(jnp.float32) * (MEM_HEAD_DIM ** -0.5)
    p = jax.nn.softmax(s, axis=-1).astype(v.dtype)
    o = jnp.einsum('bhsm,bmhd->bshd', p, v).reshape(B, S, MEM_W)
    return o @ w_o

def first_inputs(seed: int = 0) -> dict:
    key = jax.random.key(seed)
    ks = jax.random.split(key, 24)

    def dense(k, shape, fan_in):
        return jax.random.normal(k, shape, jnp.float32) * (fan_in ** -0.5)

    def gain(k, shape):
        return 1.0 + 0.02 * jax.random.normal(k, shape, jnp.float32)

    x = jax.random.normal(ks[0], (BATCH, SEQ, D_MODEL), jnp.float32)
    mem = jax.random.normal(ks[1], (BATCH, MEM_LEN, D_MODEL), jnp.float32)
    offsets = jax.random.randint(ks[2], (BATCH, 1), 0, 1024, jnp.int32)
    positions = (offsets + jnp.arange(SEQ, dtype=jnp.int32)[None, :]).astype(jnp.int32)
    L = DEPTH
    return {
        "x": x,
        "mem": mem,
        "positions": positions,
        "g_mix": gain(ks[3], (L, D_MODEL)),
        "w_in": dense(ks[4], (L, D_MODEL, IN_COLS), D_MODEL),
        "g_cq": gain(ks[5], (L, DSA_Q_RANK)),
        "w_uq": dense(ks[6], (L, DSA_Q_RANK, DSA_W), DSA_Q_RANK),
        "w_iq": dense(ks[7], (L, DSA_Q_RANK, IDX_HEADS * IDX_DIM), DSA_Q_RANK),
        "w_dsa_o": dense(ks[8], (L, DSA_W, D_MODEL), DSA_W),
        "w_moba_o": dense(ks[9], (L, MOBA_W, D_MODEL), MOBA_W),
        "w_out": dense(ks[10], (L, D_MODEL, D_MODEL), D_MODEL),
        "g_mem_q": gain(ks[11], (L, D_MODEL)),
        "g_mem_kv": gain(ks[12], (L, D_MODEL)),
        "w_mem_q": dense(ks[13], (L, D_MODEL, MEM_W), D_MODEL),
        "w_mem_kv": dense(ks[14], (L, D_MODEL, 2 * MEM_W), D_MODEL),
        "w_mem_o": dense(ks[15], (L, MEM_W, D_MODEL), MEM_W),
        "g_ff": gain(ks[16], (L, D_MODEL)),
        "w_ff1": dense(ks[17], (L, D_MODEL, D_FF), D_MODEL),
        "w_ff2": dense(ks[18], (L, D_FF, D_MODEL), D_FF),
        "g_final": gain(ks[19], (D_MODEL,)),
    }

def first_block(x, mem, positions, g_mix, w_in, g_cq, w_uq, w_iq, w_dsa_o, w_moba_o, w_out,
              g_mem_q, g_mem_kv, w_mem_q, w_mem_kv, w_mem_o, g_ff, w_ff1, w_ff2, g_final):
    pts = _split_points()
    for l in range(DEPTH):
        h = rmsnorm(x, g_mix[l])
        proj = h @ w_in[l]
        c_q, k_a, v_a, k_idx, w_idx, q_b, k_b, v_b, gl_a, gl_b = jnp.split(proj, pts, axis=-1)
        y_a = dsa_branch(c_q, k_a, v_a, k_idx, w_idx, g_cq[l], w_uq[l], w_iq[l], positions) @ w_dsa_o[l]
        y_b = moba_branch(q_b, k_b, v_b, positions) @ w_moba_o[l]
        merged = jax.nn.sigmoid(gl_a) * y_a + jax.nn.sigmoid(gl_b) * y_b
        x = x + merged @ w_out[l]
        hm = rmsnorm(x, g_mem_q[l])
        mem_n = rmsnorm(mem, g_mem_kv[l])
        x = x + mem_cross_attn(hm, mem_n, w_mem_q[l], w_mem_kv[l], w_mem_o[l])
        hf = rmsnorm(x, g_ff[l])
        x = x + jnp.square(jax.nn.relu(hf @ w_ff1[l])) @ w_ff2[l]
    return rmsnorm(x, g_final)


N_HEADS = D_MODEL // HEAD_DIM
N_FOX_HEADS = N_HEADS // 2
N_NSA_HEADS = N_HEADS - N_FOX_HEADS
NSA_GROUP = 4
NSA_KV_HEADS = N_NSA_HEADS // NSA_GROUP
D_MIX = (N_FOX_HEADS + N_NSA_HEADS) * HEAD_DIM
CMP_BLOCK = 32
CMP_STRIDE = 16
SLC_BLOCK = 64
SLC_TOPK = 16
WINDOW = 512
Q_BLOCK = 128
D_FF_2 = -(-8 * D_MODEL // (3 * 256)) * 256
RMS_EPS = 1e-6
NEG_INF = -1e30
FORCE_SCORE = 1e9

FOX_W = N_FOX_HEADS * HEAD_DIM
NSA_W = N_NSA_HEADS * HEAD_DIM
KV_W = NSA_KV_HEADS * HEAD_DIM
IN_SPLITS = (FOX_W, FOX_W, FOX_W, N_FOX_HEADS, NSA_W, KV_W, KV_W, KV_W, KV_W, KV_W, KV_W, 3 * N_NSA_HEADS)
IN_WIDTH = sum(IN_SPLITS)


def _rms_norm(x, g):
    xf = x.astype(jnp.float32)
    y = xf * lax.rsqrt(jnp.mean(xf * xf, axis=-1, keepdims=True) + RMS_EPS)
    return (y * g.astype(jnp.float32)).astype(x.dtype)

def _masked_softmax(s, mask):
    s = jnp.where(mask, s, NEG_INF)
    m = jnp.max(s, axis=-1, keepdims=True)
    p = jnp.where(mask, jnp.exp(s - m), 0.0)
    return p / jnp.maximum(jnp.sum(p, axis=-1, keepdims=True), 1e-30)

def _alibi_slopes(n):
    return jnp.exp2(-8.0 * jnp.arange(1, n + 1, dtype=jnp.float32) / n)

def _overlap_matrix(n_cmp, n_slc):
    ci = np.arange(n_cmp)[:, None]
    sj = np.arange(n_slc)[None, :]
    ov = (ci * CMP_STRIDE < (sj + 1) * SLC_BLOCK) & (ci * CMP_STRIDE + CMP_BLOCK > sj * SLC_BLOCK)
    return ov.astype(np.float32)

def _compress(tok, pos_emb, w):
    B, T, G, Dh = tok.shape
    chunks = tok.reshape(B, T // CMP_STRIDE, CMP_STRIDE, G, Dh)
    blocks = jnp.concatenate([chunks[:, :-1], chunks[:, 1:]], axis=2)
    return jnp.einsum("bnlgd,lde->bnge", blocks + pos_emb[None, None, :, None, :], w)

def _hybrid_mixer(h, w_in, fox_forget_bias, fox_q_norm, fox_k_norm, nsa_q_norm, cmp_k_norm,
                  slc_k_norm, win_k_norm, cmp_pos_k, cmp_pos_v, cmp_w_k, cmp_w_v, w_out):
    B, T, _ = h.shape
    dt = h.dtype
    f32 = jnp.float32
    Hf, Hn, G, R, Dh = N_FOX_HEADS, N_NSA_HEADS, NSA_KV_HEADS, NSA_GROUP, HEAD_DIM
    scale = HEAD_DIM ** -0.5
    n_cmp = T // CMP_STRIDE - 1
    n_slc = T // SLC_BLOCK
    k_sel = min(SLC_TOPK, n_slc)
    n_qb = T // Q_BLOCK

    proj = h @ w_in
    cuts = [int(c) for c in np.cumsum(IN_SPLITS)[:-1]]
    qf, kf, vf, ff, qn, kc, vc, ks, vs, kw, vw, gt = jnp.split(proj, cuts, axis=-1)

    qf = _rms_norm(qf.reshape(B, T, Hf, Dh), fox_q_norm)
    kf = _rms_norm(kf.reshape(B, T, Hf, Dh), fox_k_norm)
    vf = vf.reshape(B, T, Hf, Dh)
    log_f = jax.nn.log_sigmoid(ff.astype(f32) + fox_forget_bias.astype(f32))
    cum_f = jnp.transpose(jnp.cumsum(log_f, axis=1), (0, 2, 1))

    qn = _rms_norm(qn.reshape(B, T, G, R, Dh), nsa_q_norm)
    k_cmp = _rms_norm(_compress(kc.reshape(B, T, G, Dh), cmp_pos_k, cmp_w_k), cmp_k_norm)
    v_cmp = _compress(vc.reshape(B, T, G, Dh), cmp_pos_v, cmp_w_v)
    cmp_end = jnp.arange(n_cmp) * CMP_STRIDE + (CMP_BLOCK - 1)
    k_slc = jnp.transpose(_rms_norm(ks.reshape(B, n_slc, SLC_BLOCK, G, Dh), slc_k_norm), (0, 3, 1, 2, 4))
    v_slc = jnp.transpose(vs.reshape(B, n_slc, SLC_BLOCK, G, Dh), (0, 3, 1, 2, 4))
    pad = ((0, 0), (WINDOW, 0), (0, 0), (0, 0))
    k_win = jnp.pad(_rms_norm(kw.reshape(B, T, G, Dh), win_k_norm), pad)
    v_win = jnp.pad(vw.reshape(B, T, G, Dh), pad)
    gates = jax.nn.sigmoid(gt.astype(f32)).astype(dt).reshape(B, T, G, R, 3)

    slopes = _alibi_slopes(Hn).reshape(G, R)
    overlap = jnp.asarray(_overlap_matrix(n_cmp, n_slc))
    key_pos = jnp.arange(T)
    blk_ids = jnp.arange(n_slc)
    bi = jnp.arange(B)[:, None, None, None]
    gi = jnp.arange(G)[None, :, None, None]
    win_off = jnp.arange(Q_BLOCK + WINDOW) - WINDOW
    slc_off = jnp.arange(SLC_BLOCK)

    def query_block(i):
        q0 = i * Q_BLOCK
        tpos = q0 + jnp.arange(Q_BLOCK)

        qf_b = lax.dynamic_slice_in_dim(qf, q0, Q_BLOCK, axis=1)
        cq = lax.dynamic_slice_in_dim(cum_f, q0, Q_BLOCK, axis=2)
        s = jnp.einsum("bqhd,bkhd->bhqk", qf_b, kf).astype(f32) * scale
        s = s + cq[..., None] - cum_f[:, :, None, :]
        p = _masked_softmax(s, key_pos[None, :] <= tpos[:, None])
        o_fox = jnp.einsum("bhqk,bkhd->bqhd", p.astype(dt), vf)

        qn_b = lax.dynamic_slice_in_dim(qn, q0, Q_BLOCK, axis=1)

        dist_c = (tpos[:, None] - cmp_end[None, :]).astype(f32)
        s_c = jnp.einsum("bqgrd,bngd->bgrqn", qn_b, k_cmp).astype(f32) * scale
        s_c = s_c - slopes[None, :, :, None, None] * dist_c
        p_c = _masked_softmax(s_c, dist_c >= 0)
        o_c = jnp.einsum("bgrqn,bngd->bqgrd", p_c.astype(dt), v_cmp)

        imp = jnp.einsum("bgrqn,nj->bgqj", p_c, overlap)
        cur = tpos // SLC_BLOCK
        forced = (blk_ids[None, :] == 0) | (blk_ids[None, :] == cur[:, None]) | (blk_ids[None, :] == cur[:, None] - 1)
        valid = blk_ids[None, :] * SLC_BLOCK <= tpos[:, None]
        imp = jnp.where(forced, FORCE_SCORE, jnp.where(valid, imp, -FORCE_SCORE))
        _, idx = lax.top_k(imp, k_sel)
        k_g = k_slc[bi, gi, idx]
        v_g = v_slc[bi, gi, idx]
        spos = idx[..., None] * SLC_BLOCK + slc_off
        dist_s = (tpos[None, None, :, None, None] - spos).astype(f32)[:, :, None]
        s_s = jnp.einsum("bqgrd,bgqkld->bgrqkl", qn_b, k_g).astype(f32) * scale
        s_s = s_s - slopes[None, :, :, None, None, None] * dist_s
        flat = (B, G, R, Q_BLOCK, k_sel * SLC_BLOCK)
        mask_s = jnp.broadcast_to(dist_s >= 0, s_s.shape).reshape(flat)
        p_s = _masked_softmax(s_s.reshape(flat), mask_s).reshape(s_s.shape)
        o_s = jnp.einsum("bgrqkl,bgqkld->bqgrd", p_s.astype(dt), v_g)

        k_wb = lax.dynamic_slice_in_dim(k_win, q0, Q_BLOCK + WINDOW, axis=1)
        v_wb = lax.dynamic_slice_in_dim(v_win, q0, Q_BLOCK + WINDOW, axis=1)
        wpos = q0 + win_off
        dist_w = tpos[:, None] - wpos[None, :]
        mask_w = (dist_w >= 0) & (dist_w < WINDOW) & (wpos[None, :] >= 0)
        s_w = jnp.einsum("bqgrd,bkgd->bgrqk", qn_b, k_wb).astype(f32) * scale
        s_w = s_w - slopes[None, :, :, None, None] * dist_w.astype(f32)
        p_w = _masked_softmax(s_w, mask_w)
        o_w = jnp.einsum("bgrqk,bkgd->bqgrd", p_w.astype(dt), v_wb)

        g_b = lax.dynamic_slice_in_dim(gates, q0, Q_BLOCK, axis=1)
        o_nsa = g_b[..., 0:1] * o_c + g_b[..., 1:2] * o_s + g_b[..., 2:3] * o_w
        return o_fox, o_nsa.reshape(B, Q_BLOCK, Hn, Dh)

    o_fox, o_nsa = lax.map(query_block, jnp.arange(n_qb))
    o_fox = jnp.moveaxis(o_fox, 0, 1).reshape(B, T, FOX_W)
    o_nsa = jnp.moveaxis(o_nsa, 0, 1).reshape(B, T, NSA_W)
    return jnp.concatenate([o_fox, o_nsa], axis=-1) @ w_out

def _swiglu(h, w_gate, w_up, w_down):
    return (jax.nn.silu(h @ w_gate) * (h @ w_up)) @ w_down

def second_inputs(seed: int = 0) -> dict:
    key = jax.random.key(seed)
    ks = jax.random.split(key, 20)
    f32 = jnp.float32
    nrm = lambda k, shape, s: jax.random.normal(k, shape, f32) * s
    gain = lambda k, shape: 1.0 + 0.02 * jax.random.normal(k, shape, f32)
    L = DEPTH
    return {
        "x": nrm(ks[0], (BATCH, SEQ, D_MODEL), 1.0),
        "attn_norm": gain(ks[1], (L, D_MODEL)),
        "w_in": nrm(ks[2], (L, D_MODEL, IN_WIDTH), D_MODEL ** -0.5),
        "fox_forget_bias": 3.0 + 0.5 * jax.random.normal(ks[3], (L, N_FOX_HEADS), f32),
        "fox_q_norm": gain(ks[4], (L, HEAD_DIM)),
        "fox_k_norm": gain(ks[5], (L, HEAD_DIM)),
        "nsa_q_norm": gain(ks[6], (L, HEAD_DIM)),
        "cmp_k_norm": gain(ks[7], (L, HEAD_DIM)),
        "slc_k_norm": gain(ks[8], (L, HEAD_DIM)),
        "win_k_norm": gain(ks[9], (L, HEAD_DIM)),
        "cmp_pos_k": nrm(ks[10], (L, CMP_BLOCK, HEAD_DIM), 0.02),
        "cmp_pos_v": nrm(ks[11], (L, CMP_BLOCK, HEAD_DIM), 0.02),
        "cmp_w_k": nrm(ks[12], (L, CMP_BLOCK, HEAD_DIM, HEAD_DIM), (CMP_BLOCK * HEAD_DIM) ** -0.5),
        "cmp_w_v": nrm(ks[13], (L, CMP_BLOCK, HEAD_DIM, HEAD_DIM), (CMP_BLOCK * HEAD_DIM) ** -0.5),
        "w_out": nrm(ks[14], (L, D_MIX, D_MODEL), D_MIX ** -0.5),
        "ffn_norm": gain(ks[15], (L, D_MODEL)),
        "w_gate": nrm(ks[16], (L, D_MODEL, D_FF_2), D_MODEL ** -0.5),
        "w_up": nrm(ks[17], (L, D_MODEL, D_FF_2), D_MODEL ** -0.5),
        "w_down": nrm(ks[18], (L, D_FF_2, D_MODEL), D_FF_2 ** -0.5),
    }

def second_block(x, attn_norm, w_in, fox_forget_bias, fox_q_norm, fox_k_norm, nsa_q_norm, cmp_k_norm,
              slc_k_norm, win_k_norm, cmp_pos_k, cmp_pos_v, cmp_w_k, cmp_w_v, w_out, ffn_norm,
              w_gate, w_up, w_down):
    for l in range(DEPTH):
        h = _rms_norm(x, attn_norm[l])
        x = x + _hybrid_mixer(h, w_in[l], fox_forget_bias[l], fox_q_norm[l], fox_k_norm[l], nsa_q_norm[l],
                              cmp_k_norm[l], slc_k_norm[l], win_k_norm[l], cmp_pos_k[l], cmp_pos_v[l],
                              cmp_w_k[l], cmp_w_v[l], w_out[l])
        h = _rms_norm(x, ffn_norm[l])
        x = x + _swiglu(h, w_gate[l], w_up[l], w_down[l])
    return x


def setup_inputs(seed=0):
    out = dict(first_inputs(seed))
    for name, value in second_inputs(seed + 1).items():
        if name != "x":
            out[name + "_2"] = value
    return out


def reference(
    x, mem, positions, g_mix, w_in, g_cq, w_uq, w_iq, w_dsa_o, w_moba_o, w_out, g_mem_q,
    g_mem_kv, w_mem_q, w_mem_kv, w_mem_o, g_ff, w_ff1, w_ff2, g_final, attn_norm_2, w_in_2,
    fox_forget_bias_2, fox_q_norm_2, fox_k_norm_2, nsa_q_norm_2, cmp_k_norm_2, slc_k_norm_2,
    win_k_norm_2, cmp_pos_k_2, cmp_pos_v_2, cmp_w_k_2, cmp_w_v_2, w_out_2, ffn_norm_2, w_gate_2,
    w_up_2, w_down_2,
):
    x = first_block(
        x, mem, positions, g_mix, w_in, g_cq, w_uq, w_iq, w_dsa_o, w_moba_o, w_out, g_mem_q,
        g_mem_kv, w_mem_q, w_mem_kv, w_mem_o, g_ff, w_ff1, w_ff2, g_final,
    )
    return second_block(
        x, attn_norm_2, w_in_2, fox_forget_bias_2, fox_q_norm_2, fox_k_norm_2, nsa_q_norm_2,
        cmp_k_norm_2, slc_k_norm_2, win_k_norm_2, cmp_pos_k_2, cmp_pos_v_2, cmp_w_k_2,
        cmp_w_v_2, w_out_2, ffn_norm_2, w_gate_2, w_up_2, w_down_2,
    )


_drawn_inputs = setup_inputs


def setup_inputs(seed=0):
    import zlib

    import numpy as np

    out = dict(_drawn_inputs(seed))
    spreads = {}
    factors = {'g_mix': 3.197,
     'g_cq': 4.022,
     'g_mem_q': 8.0,
     'g_mem_kv': 8.0,
     'g_ff': 2.864,
     'attn_norm_2': 4.362,
     'fox_q_norm_2': 8.0,
     'fox_k_norm_2': 8.0,
     'nsa_q_norm_2': 8.0,
     'cmp_k_norm_2': 8.0,
     'slc_k_norm_2': 8.0,
     'win_k_norm_2': 8.0,
     'cmp_pos_k_2': 30.991,
     'cmp_pos_v_2': 21.368,
     'ffn_norm_2': 4.322}
    for name, (base, spread) in spreads.items():
        noise = np.random.default_rng([zlib.crc32(name.encode()), seed]).standard_normal(out[name].shape)
        drawn = base * np.exp(spread * noise) if base else spread * noise
        out[name] = __import__('jax').numpy.asarray(drawn.astype(out[name].dtype))
    for name, factor in factors.items():
        out[name] = (out[name] * factor).astype(out[name].dtype)
    return out
```

```python
from contextlib import ExitStack

import numpy as np

import concourse.bass as bass
from concourse import mybir

F32 = mybir.dt.float32
F32R = mybir.dt.float32r
I32 = mybir.dt.int32
ALU = mybir.AluOpType
ACT = mybir.ActivationFunctionType
AX = mybir.AxisListType

P = 128
SEQ = 256
NT = SEQ // P
D = 2048
KT = D // P
CH = 512
HD = 128
EPS = 1e-6
NEG = -1e30
FAR = 1e33
TAKEN = -3.0e38
SCALE = HD ** -0.5
TOPK = min(256, SEQ // 4)
IDX_H, IDX_D = 16, 64
W_IDX_SCALE = IDX_H ** -0.5 * IDX_D ** -0.5
ROPE_HALF = 16
THETA = 500000.0
FF = 8192
FF2 = 5632
RING = 4
GROUP = 2 * CH
CMP_N, CMP_STRIDE, CMP_LEN = 15, 16, 32
NSA_HEADS, KV_HEADS = 8, 2
SLOPES = [2.0 ** (-8.0 * (h + 1) / NSA_HEADS) for h in range(NSA_HEADS)]
MAGIC = 12582912.0
TWO_PI = (6.28125, float(np.float32(2 * np.pi - 6.28125) - np.float32(2 * np.pi - 6.28125) % np.float32(2.0 ** -20)))
TWO_PI = TWO_PI + (2 * np.pi - TWO_PI[0] - TWO_PI[1],)
PI_IN = 3.1415925

CQ, KA, VA, KIDX, QB, KB, VB, GLA, GLB = 0, 512, 1536, 2560, 2640, 3664, 4688, 5712, 7760
QF, KF, VF, FG, QN, KC, KS, KW, GT = 0, 1024, 2048, 3072, 3080, 4104, 4616, 5128, 5640

G_ROWS = {"g_mix": 0, "g_mem_q": 16, "g_mem_kv": 32, "g_ff": 48, "attn_norm_2": 64, "ffn_norm_2": 80,
          "g_cq": 96, "fox_q_norm_2": 100, "fox_k_norm_2": 101, "nsa_q_norm_2": 102, "cmp_k_norm_2": 103,
          "slc_k_norm_2": 104, "win_k_norm_2": 105, "g_final": 106}
N_GROWS = 122


def gemm(w, row0, col0, kt, src, k0=0, width=CH, need=(), rows=False, step=(0, 0), cols2=None, kind="gemm", gk=2, **more):
    return dict(w=w, row0=row0, col0=col0, kt=kt, src=src, k0=k0, n=width, need=need, rows=rows, step=step,
                cols2=cols2, kind=kind, gk=gk, count=4 if kind == "cmp" else kt // gk, **more)


def groups_of(c):
    return [("G", dict(chunk=c, i=i)) for i in range(c["count"])]


def weave(c, side=(), start=1):
    main, side = groups_of(c), list(side)
    slots = len(main) - start + 1
    out, done = [], 0
    for i, item in enumerate(main):
        out.append(item)
        if i + 1 >= start:
            want = -(-len(side) * (i + 2 - start) // slots)
            out += side[done:want]
            done = want
    out += side[done:] + [("E", c)]
    return [x for item in out for x in (item if isinstance(item, list) else [item])]


def lead(c, steps, ahead=2):
    out = list(steps[:ahead])
    for i, item in enumerate(groups_of(c)):
        out += [item] + list(steps[ahead + i:ahead + i + 1])
    return out + [("E", c)]


def turn(src, col, to, k, rows, **more):
    return ("T", dict(src=src, col=col, to=to, k=k, rows=rows, **more))


def turns(c, to, k, **more):
    return [turn("stage", 2 * i * P, to, k + 2 * i, c, **more) for i in range(2)]


def filled(steps):
    return [(what["k"], what) for _, what in steps]


def attention(units):
    out, m, values = [], len(units), []
    for i in range(m + 2):
        one, two = [], []
        if 1 <= i <= m:
            one.append(("N", units[i - 1]))
            two.append(("P", dict(unit=units[i - 1], slot=(i - 1) % 3)))
        if i < m:
            one.append(("S", units[i]))
        if i >= 2:
            values.append(("O", dict(units=[units[i - 2]], slots=[(i - 2) % 3], k=units[i - 2]["k"])))
            two.append(values[-1])
        out += [x for x in (one, two) if x]
    return out, values


def nsa_attention(units):
    out, m, values = [], len(units), []
    for i in range(m + 1):
        one, two = [], []
        if i >= 1:
            one.append(("N", units[i - 1]))
            two.append(("P", dict(unit=units[i - 1], slot=(i - 1) % 3)))
        if i < m:
            one.append(("S", units[i]))
        if i % 3 == 1 and i > 1:
            values.append(("O", dict(units=units[i - 4:i - 1], slots=[0, 1, 2], k=8 + i // 3 - 1)))
            two.insert(0, values[-1])
        out += [x for x in (one, two) if x]
    values.append(("O", dict(units=units[m - 3:m], slots=[0, 1, 2], k=8 + m // 3 - 1)))
    out.append([values[-1]])
    return out, values


def cut(steps, n):
    return [steps[i * len(steps) // n:(i + 1) * len(steps) // n] for i in range(n)]


def plan():
    rows_x = dict(r_fixed=0)

    xt = [turn("x", 2 * i * P, "A", 2 * i, rows_x, gain="g_mix") for i in range(8)]
    seq = [("init", {}), ("V", dict(which=0))]

    def w_in(col, ev, **more):
        return gemm("w_in", 0, col, KT, "A", ev=ev, rstd="h", **more)

    cq = gemm("w_in", 0, CQ, KT, "A", need=filled(xt), ev="cq", rstd="h", rows=True)
    first = lead(cq, xt)
    seq += first[:-1] + [("V", dict(which=1)), ("V", dict(which=2)), ("rope", {}), ("rstd", dict(of="x", name="h", first=True)), first[-1]]
    cqt = turns(cq, "B", 12, gain="g_cq", gain_k=0)
    ka0 = w_in(KA, "rope", rows=True)
    seq += weave(ka0, cqt, 3)
    ka1 = w_in(KA + CH, "rope", rows=True)
    seq += weave(ka1, turns(ka0, "ka", 0), 3)
    idx = w_in(KIDX, "idx", width=80, rows=True, gk=8)
    seq += weave(idx)
    va0, va1 = [w_in(VA + i * CH, "value", to="va", off=i * CH) for i in range(2)]
    seq += weave(va0, turns(ka1, "ka", 4) + [turn("stage", 0, "kidx", 0, idx, one=True)], 2) + weave(va1)
    qi = [gemm("w_iq", 0, i * CH, 4, "B", 12, need=[(k - 12, t) for k, t in filled(cqt)] if i == 0 else (),
               ev="ropei", rstd="cq", rows=True) for i in range(2)]
    kb = [w_in(KB + i * CH, "rope", rows=True) for i in range(2)]
    seq += weave(qi[0]) + weave(qi[1])
    seq += weave(kb[0], turns(qi[0], "qi", 0) + turns(qi[1], "qi", 4), 2)
    index = [("X", dict(t=0, heads=[h0, h0 + 2, h0 + 4, h0 + 6])) for h0 in (0, 1, 8, 9)]
    index += [("X", dict(t=1, heads=[h0, h0 + 2])) for h0 in (0, 1, 4, 5, 8, 9, 12, 13)] 
    index += [("K", dict(t=t, part=i)) for t in range(NT) for i in range(4)]
    seq += weave(kb[1], turns(kb[0], "kb", 0) + index[:10], 2)
    qa = [gemm("w_uq", 0, i * CH, 4, "B", 12, ev="rope", rstd="cq", rows=True) for i in range(2)]
    vb = [w_in(VB + i * CH, "value", to="vb", off=i * CH) for i in range(2)]
    seq += weave(qa[0], turns(kb[1], "kb", 4))
    seq += weave(vb[0], turns(qa[0], "qa", 0, scale=SCALE) + index[10:], 2)
    seq += weave(qa[1])
    seq += weave(vb[1], turns(qa[1], "qa", 4, scale=SCALE), 5)
    dsa = [dict(kind="dsa", q="qa", kk="ka", v="va", h=h, kh=h, k=h) for h in range(8)]
    steps, o_dsa = attention(dsa)
    part = cut(steps, 2)
    qb = [w_in(QB + i * CH, "rope", rows=True) for i in range(2)]
    seq += weave(qb[0], part[0], 1)
    seq += weave(qb[1], turns(qb[0], "qb", 0, scale=SCALE) + part[1], 2)
    moba = [dict(kind="moba", q="qb", kk="kb", v="vb", h=h, kh=h, k=8 + h) for h in range(8)]
    steps, o_moba = attention(moba)
    part = cut(steps, 4)
    part[0] = turns(qb[1], "qb", 4, scale=SCALE) + part[0]
    for i in range(4):
        seq += weave(w_in(GLA + i * CH, "gate", to="sa", off=i * CH), part[i], 3 if i == 0 else 1)
    glb = [w_in(GLB + i * CH, "gate", to="sb", off=i * CH) for i in range(4)]
    seq += weave(glb[0]) + [("load_mem", dict(after=o_moba[-1][1]))]
    seq += weave(glb[1]) + weave(glb[2], [("rstd", dict(of="mem", name="mem"))]) + weave(glb[3])

    pend, merged = [], []
    for i in range(4):
        ya = gemm("w_dsa_o", 0, i * CH, 8, "B", 0, need=filled(o_dsa) if i == 0 else (), ev="ya", off=i * CH)
        yb = gemm("w_moba_o", 0, i * CH, 8, "B", 8, need=[(k - 8, o) for k, o in filled(o_moba)] if i == 0 else (), ev="yb", off=i * CH, rows=True)
        seq += weave(ya, pend, 3) + weave(yb)
        pend = [turn("sa", i * CH + 2 * k * P, "A", 4 * i + 2 * k, yb) for k in range(2)]
        merged += pend
    mt = [turn("mem", 2 * i * P, "B", 2 * i, rows_x, gain="g_mem_kv") for i in range(8)]
    side = [pend, mt[0:3], mt[3:6], mt[6:8]]
    wo = [gemm("w_out", 0, i * CH, KT, "A", need=filled(merged) if i == 0 else (), ev="addx", off=i * CH, rows=True)
          for i in range(4)]
    for i in range(4):
        seq += weave(wo[i], side[i], 2 if i == 0 else 1)

    hm = [turn("x", 2 * i * P, "A", 2 * i, wo[i // 2], gain="g_mem_q") for i in range(8)]
    km = gemm("w_mem_kv", 0, 0, KT, "B", need=filled(mt), ev="plain", rstd="mem", rows=True)
    seq += weave(km, hm, 1) + [("rstd", dict(of="x", name="h"))]
    mq = gemm("w_mem_q", 0, 0, KT, "A", need=filled(hm), ev="plain", rstd="h", rows=True)
    vm = gemm("w_mem_kv", 0, CH, KT, "B", ev="value", to="vm", off=0, rstd="mem")
    steps, o_mem = attention([dict(kind="mem", q="qm", kk="km", v="vm", h=h, kh=h, k=h) for h in range(4)])
    seq += weave(mq, turns(km, "km", 0), 3) + weave(vm, turns(mq, "qm", 0, scale=SCALE) + steps[:4] + [steps[4][:1]], 2)
    seq += steps[4][1:] + [x for step in steps[5:] for x in step]
    pend, hf = [], []
    for i in range(4):
        mo = gemm("w_mem_o", 0, i * CH, 4, "B", 0, need=filled(o_mem) if i == 0 else (), ev="addx", off=i * CH, rows=True)
        seq += weave(mo, pend, 2)
        pend = [turn("x", i * CH + 2 * k * P, "A", 4 * i + 2 * k, mo, gain="g_ff") for k in range(2)]
        hf += pend

    def up(i, half, **more):
        return gemm("w_ff1", 0, (2 * i + half) * CH, KT, "A", ev="relu2", rstd="h", step=(0, 2 * CH), rows=True, **more)

    fa, fb = up(0, 0, need=filled(hf)), up(0, 1)
    seq += weave(fa, pend + [("rstd", dict(of="x", name="h"))], 2)
    ta = turns(fa, "B", 0)
    seq += weave(fb, ta, 3)
    segments = [(seq, 1)]
    body = []
    tb = turns(fb, "B", 4)
    fa, fb2 = up(1, 0), up(1, 1)
    body += weave(fa, tb, 3)
    down_need = filled(ta + tb)
    for m in range(4):
        body += weave(gemm("w_ff2", 0, m * CH, 8, "B", 0, need=down_need if m == 0 else (), ev="addx", off=m * CH,
                           step=(2 * CH, 0)))
    ta2 = turns(fa, "B", 0)
    body += weave(fb2, ta2, 2)
    turns_ff = FF // (2 * CH)
    segments.append((body, turns_ff - 1))

    tb = turns(fb2, "B", 4)
    seq, xt = tb + [("load_gain", {})], []
    pend = []
    for m in range(4):
        c = gemm("w_ff2", (turns_ff - 1) * 2 * CH, m * CH, 8, "B", 0, need=filled(ta2 + tb) if m == 0 else (),
                 ev="addx", off=m * CH, rows=True, twice=True)
        seq += weave(c, pend, 2)
        pend = [turn("x", m * CH + 2 * k * P, "A", 4 * m + 2 * k, c, gain="attn_norm_2") for k in range(2)]
        xt += pend

    def w_in2(col, ev, **more):
        return gemm("w_in_2", 0, col, KT, "A", ev=ev, rstd="h", **more)

    qn = [w_in2(QN + i * CH, "hnorm", heads=4, rows=True, need=filled(xt) if i == 0 else ()) for i in range(2)]
    kc, ks, kw = w_in2(KC, "plain", rows=True), w_in2(KS, "kv", to="vs", rows=True), w_in2(KW, "kv", to="vw", rows=True)
    seq += weave(qn[0], pend + [("rstd", dict(of="x", name="f")), ("rstd", dict(of="x2", name="h"))], 2)
    seq += [("renorm", dict(m=m)) for m in range(4)]
    seq += weave(kc, turns(qn[0], "qn", 0, scale=SCALE, hgain="nsa_q_norm_2"), 3)
    seq += weave(ks, [turn("stage", 0, "kc", 0, kc), turn("stage", 2 * P, "vc", 0, kc)], 3)
    seq += [("blocks", dict(of="kc", k=0)), ("blocks", dict(of="vc", k=8))]
    seq += weave(kw, [turn("stage", 0, "ks", 0, ks, hgain="slc_k_norm_2")], 3)
    cmpk = gemm("cmp_w_k_2", 0, 0, 0, "B", 0, kind="cmp", ev="cmpk", rows=True)
    cmpv = gemm("cmp_w_v_2", 0, 0, 0, "B", 8, kind="cmp", ev="cmpv")
    fg = w_in2(FG, "fg", width=32, cols2=(8, GT), rows=True, gk=16)
    seq += weave(qn[1], [turn("stage", 0, "kw", 0, kw, hgain="win_k_norm_2")], 3)
    seq += weave(cmpk) + weave(cmpv) + weave(fg)
    tq = turns(qn[1], "qn", 4, scale=SCALE, hgain="nsa_q_norm_2")
    cum = [("C", dict(which=0, rows=fg)), ("C", dict(which=1, rows=fg))]
    units = []
    for h in range(NSA_HEADS):
        kh = h // (NSA_HEADS // KV_HEADS)
        units += [dict(kind="cmp", q="qn", kk="kcmp", v="vcmp", h=h, kh=0, g=kh, b=0),
                  dict(kind="alibi", q="qn", kk="ks", v="vs", h=h, kh=kh, b=1),
                  dict(kind="alibi", q="qn", kk="kw", v="vw", h=h, kh=kh, b=2)]
    steps, o_nsa = nsa_attention(units)
    part = cut(steps, 6)
    pend = tq + [("T", dict(src="kcmp", col=0, to="kcmp", k=0, rows=cmpk, one=True))] + cum
    for i in range(2):
        for name, col, gain, scale in (("qf", QF, "fox_q_norm_2", SCALE), ("kf", KF, "fox_k_norm_2", None), ("vf", VF, None, None)):
            m = i * 3 + "qkv".index(name[0])
            if name == "vf":
                c = w_in2(col + i * CH, "value", to="vf", off=i * CH)
            else:
                c = w_in2(col + i * CH, "hnorm", heads=4, rows=True)
            seq += weave(c, pend + part[m], 3)
            pend = [] if name == "vf" else turns(c, name, 4 * i, hgain=gain, scale=scale)
    steps, o_fox = attention([dict(kind="fox", q="qf", kk="kf", v="vf", h=h, kh=h, k=h) for h in range(8)])
    part = cut(steps, 4)
    for i in range(4):
        seq += weave(gemm("w_out_2", 1024, i * CH, 8, "B", 8, need=[(k - 8, o) for k, o in filled(o_nsa)] if i == 0 else (), ev="addx", off=i * CH, rows=True), part[i], 1)
    pend, hf = [], []
    for i in range(4):
        wf = gemm("w_out_2", 0, i * CH, 8, "B", 0, need=filled(o_fox) if i == 0 else (), ev="addx", off=i * CH, rows=True)
        seq += weave(wf, pend, 3)
        pend = [turn("x", i * CH + 2 * k * P, "A", 4 * i + 2 * k, wf, gain="ffn_norm_2") for k in range(2)]
        hf += pend

    def gate(i, **more):
        return gemm("w_gate_2", 0, i * CH, KT, "A", ev="silu", rstd="h", step=(0, CH), **more)

    def up2(i):
        return gemm("w_up_2", 0, i * CH, KT, "A", ev="glu", rstd="h", step=(0, CH), rows=True)

    u0, u1 = up2(0), up2(1)
    seq += weave(gate(0, need=filled(hf)), pend + [("rstd", dict(of="x", name="h"))], 2) + weave(u0)
    segments.append((seq, 1))
    tg = [turn("prod", 2 * k * P, "B", 2 * k, u0) for k in range(2)]
    body = weave(gate(1), tg, 3) + weave(u1)
    for m in range(4):
        body += weave(gemm("w_down_2", 0, m * CH, 4, "B", 0, need=filled(tg) if m == 0 else (), ev="addx", off=m * CH,
                           step=(CH, 0)))
    segments.append((body, FF2 // CH - 1))
    tg = [turn("prod", 2 * k * P, "B", 2 * k, u1) for k in range(2)]
    seq, stores = list(tg), []
    for m in range(4):
        c = gemm("w_down_2", FF2 - CH, m * CH, 4, "B", 0, need=filled(tg) if m == 0 else (), ev="addx", off=m * CH, rows=True)
        seq += weave(c)
        stores.append(("store", dict(m=m, rows=c)))
    seq += stores
    segments.append((seq, 1))
    return segments


COUNTS = "gcjurs"


def number(segments):
    n = dict.fromkeys(COUNTS, 0)
    groups, landed, out = [], [0] * RING, []

    def take(what, key):
        what[key], what["ref_" + key] = n[key], n[key]
        n[key] += 1
        return what

    for items, reps in segments:
        start, mine, at = dict(n), [], len(groups)
        for kind, what in items:
            if kind == "G":
                c = what["chunk"]
                if what["i"] == 0:
                    take(c, "c")
                    mine.append(c)
                take(what, "g")
                tiles = range(c["gk"] * what["i"], c["gk"] * (what["i"] + 1))
                what["need_j"] = [x["ref_j"] for k, x in c["need"] if k in tiles]
                s = what["g"] % RING
                landed[s] += 32 if c["cols2"] else 16
                groups.append(dict(chunk=c, i=what["i"], landed=landed[s], width=GROUP if c["kind"] == "cmp" else c["gk"] * c["n"]))
                c["end"] = what["g"] + 1
            elif kind in "TPOXCV":
                take(what, "j")
            elif kind == "S":
                take(what, "u")
            if kind == "E" and what["rows"]:
                if what.get("ev") not in ("plain", "glu"):
                    n["r"] += 1
                    what["r"] = what["ref_r"] = n["r"]
                if what.get("ev") in STAGED:
                    take(what, "s")
            if "rows" in what and isinstance(what["rows"], dict):
                what["rows_r"] = what["rows"].get("r_fixed", what["rows"].get("ref_r"))
                what["rows_s"] = what["rows"].get("ref_s")
                what["rows_c"] = what["rows"].get("ref_c") if what["rows"].get("ev") in ("plain", "glu") else None
            if kind == "load_mem":
                what["after_j"] = what["after"]["ref_j"]
            mine.append(what)
        per = {k: n[k] - start[k] for k in COUNTS}
        if reps > 1:
            assert per["g"] % RING == per["c"] % 2 == per["j"] % 2 == per["s"] % 2 == 0
            seen = set()
            for what in mine:
                for k in COUNTS:
                    if "ref_" + k in what and (id(what), k) not in seen:
                        seen.add((id(what), k))
                        what["ref_" + k] += per[k] * (reps - 1)
            turn_groups = groups[at:]
            for t in range(1, reps):
                groups += [dict(x, landed=x["landed"] + t * per["g"] // RING * 16) for x in turn_groups]
            landed = [x + (reps - 1) * per["g"] // RING * 16 for x in landed]
            for k in COUNTS:
                n[k] += per[k] * (reps - 1)
        out.append((items, reps, per))
    return out, groups


STAGED = {"cq", "rope", "ropei", "idx", "plain", "hnorm", "kv", "relu2"}


class Turn:

    def __init__(self, i=0, per=None):
        per = per or dict.fromkeys(COUNTS, 0)
        self.g, self.r, self.i = i * per["g"], i * per["r"], i
        self.lo = [i * (per["g"] // RING * 3)] * 3 + [i * (per["g"] // RING)]
        self.landed = i * (per["g"] // RING * 16)
        self.c2, self.j2, self.steps = i * (per["c"] // 2), i * (per["j"] // 2), 0


def lo_count(g):
    return g // RING + 1 if g % RING == RING - 1 else g // RING * 3 + g % RING + 1


def wait(eng, sem, n, moved=0):
    if n > 0 or not isinstance(moved, int):
        assert n > 0
        eng.wait_ge(sem, n + moved)


def two_blocks(nc, a, out):
    segments, groups = number(plan())
    ctx = ExitStack()
    with ctx:
        def sb(name, shape, dt=F32):
            return ctx.enter_context(nc.sbuf_tensor(name, shape, dt))

        def sem(name):
            return ctx.enter_context(nc.semaphore(name))

        xres = sb("xres", [P, NT, D])
        act = {"A": [sb("act_a_hi", [P, KT * SEQ], F32R), sb("act_a_lo", [P, KT * SEQ], F32R)],
               "B": [sb("act_b_hi", [P, KT * SEQ + 64], F32R), sb("act_b_lo", [P, KT * SEQ + 64], F32R)]}
        raw = sb("w_raw", [P, RING, GROUP])
        whi = sb("w_hi", [P, RING, GROUP], F32R)
        wlo = sb("w_lo", [P, RING, GROUP], F32R)
        heads = sb("heads", [P, 12288])
        stage = sb("stage", [P, 2, NT, CH])
        s_sb = sb("s_sb", [P, 2, 512])
        pt_sb = sb("pt_sb", [P, 9 * P])
        scratch = sb("scratch", [P, CH])
        ident = sb("ident", [P, P])
        tri_ones = sb("tri_ones", [P, 2 * P])
        causal = sb("causal", [P, 3 * P])
        misc = sb("misc", [P, 8 * P])
        picked, score, kidx = misc[:, 0:3 * P], misc[:, 3 * P:6 * P], misc[:, 6 * P:8 * P]
        dist = misc[:, 0:3 * P]
        dist_cmp = misc[:, 3 * P:5 * P].rearrange("p (g t n) -> p g t n", g=KV_HEADS, t=NT)
        seen_cmp = misc[:, 5 * P:7 * P].rearrange("p (g t n) -> p g t n", g=KV_HEADS, t=NT)
        gains = sb("gains", [P, P])
        pos_emb = sb("pos_emb", [P, 64])
        inv = sb("inv", [P, ROPE_HALF])
        trig = sb("trig", [P, 2, NT, 2 * ROPE_HALF])
        trig8 = sb("trig8", [P, 2, NT, ROPE_HALF])
        sm = sb("small", [P, 512])
        posi = sb("posi", [P, NT], I32)
        newton_i = sb("newton_i", [P, 16], I32)
        cum_t = sb("cum_t", [8, SEQ])
        g_rows, p_rows = stage[:, 0, 0, 0:P], stage[0:64, 0, 0, P:2 * P]
        iota_i = pt_sb[:, 0:3 * P].bitcast(I32)
        bank = [ctx.enter_context(nc.psum_tensor(f"bank{i}", [P, 512], F32)) for i in range(8)]
        prod_bank, aux_bank, s_bank = bank[0:4], bank[4:6], bank[6:8]

        at = {}

        def small(name, n):
            at[name] = (at["_end"], at["_end"] + n) if "_end" in at else (0, n)
            at["_end"] = at[name][1]
            assert at["_end"] <= 512

        for name, n in (("ss", 8), ("rstd_h", 2), ("half_h", 2), ("rstd_mem", 2), ("rstd_cq", 2), ("ss_cq", 2), ("ms", 16), ("y", 16),
                        ("t1", 16), ("hss", 16), ("hrstd", 16), ("nmax", 4), ("rsum", 4), ("rinv", 4), ("top", 8),
                        ("w_idx", 32), ("ang", 32), ("turns", 32), ("red", 32), ("sin_in", 32), ("logit", 16), ("e16", 16),
                        ("logf", 16), ("gate", 48), ("cum_q", 16), ("posf", 2), ("bias", 8), ("ss2", 8), ("rstd_f", 2), ("rm", 4)):
            small(name, n)

        def s_(name, lo=0, hi=None):
            b, e = at[name]
            return sm[:, b + lo:(e if hi is None else b + hi)]

        def part(name, off, *shape):
            n = int(np.prod(shape))
            v = heads[:, off:off + n]
            return v.rearrange("p (a b) -> p a b", a=shape[0]) if len(shape) == 2 else v

        qk = {"ka": part("ka", 0, 8, SEQ), "qa": part("qa", 2048, 8, SEQ), "kb": part("kb", 4096, 8, SEQ),
              "qb": part("qb", 6144, 8, SEQ), "qi": part("qi", 6144, 8, SEQ),
              "km": part("km", 0, 4, SEQ), "qm": part("qm", 1024, 4, SEQ),
              "qn": part("qn", 0, 8, SEQ), "kc": part("kc", 2048, 2, SEQ), "vc": part("vc", 2560, 2, SEQ),
              "ks": part("ks", 3072, 2, SEQ), "kw": part("kw", 3584, 2, SEQ), "kcmp": part("kcmp", 5120, 1, 64),
              "qf": part("qf", 6144, 8, SEQ), "kf": part("kf", 8192, 8, SEQ)}
        val = {"va": part("va", 8192, NT, 1024), "vb": part("vb", 10240, NT, 1024), "vm": part("vm", 2048, NT, CH),
               "vs": part("vs", 4096, NT, 256), "vw": part("vw", 4608, NT, 256), "vf": part("vf", 10240, NT, 1024),
               "sa": part("sa", 0, NT, D), "sb": part("sb", 4096, NT, D), "mem": part("mem", 8192, NT, D), "x": xres}
        v_cmp = heads[0:64, 5184:5312]
        k_cmp = heads[0:64, 5312:5440]
        cmp_junk = heads[0:64, 5440:5568]
        gain_rows = heads[:, 6144:6144 + D]
        blk_sum = heads[:, 6144:6144 + 2048]
        rel = s_sb

        x_landed = [sem(f"x_landed{m}") for m in range(4)]
        gmix_landed, small_landed, mem_landed, gain_landed = map(sem, ("gmix_landed", "small_landed", "mem_landed", "gain_landed"))
        w_landed = [sem(f"w_landed{i}") for i in range(RING)]
        hi_ready, group_done = sem("hi_ready"), sem("group_done")
        lo_pool, lo_dve = sem("lo_pool"), sem("lo_dve")
        lo_ready = [lo_pool] * 3 + [lo_dve]
        chunk_out = [sem("chunk_out0"), sem("chunk_out1")]
        aux_done = sem("aux_done")
        aux_out = [sem("aux_out0"), sem("aux_out1")]
        rows_ready = sem("rows_ready")
        scores_done, row_max_ready, exp_done, probs_ready = map(sem, ("scores_done", "row_max_ready", "exp_done", "probs_ready"))
        scored = sem("scored")
        consts_ready, alibi_ready = sem("consts_ready"), sem("alibi_ready")
        angle_ready, sine_ready = sem("angle_ready"), sem("sine_ready")
        forget_in, forget_act, gate_act = sem("forget_in"), sem("forget_act"), sem("gate_act")
        dve_step, act_step, pool_step = sem("dve_step"), sem("act_step"), sem("pool_step")
        rstd_ready, blocks_ready = sem("rstd_ready"), sem("blocks_ready")
        stored = sem("stored")

        def pt_of(unit, slot):
            return pt_sb[:, unit["u"] % 2 * 512:unit["u"] % 2 * 512 + 512] if unit["kind"] == "mem" else pt_sb[:, slot * 3 * P:(slot + 1) * 3 * P]

        def weights(c, i, turn):
            w = a[c["w"]]
            if c["kind"] == "cmp":
                return [((0, GROUP), w[0, 8 * i:8 * i + 8].rearrange("l d e -> d l e"), "l")]
            size = c["gk"] * P
            r, col = c["row0"] + size * i, c["col0"]
            rows, cols = slice(r, r + size), slice(col, col + c["n"])
            if not isinstance(turn.i, int):
                if c["step"][0]:
                    rows = bass.ds(turn.i * c["step"][0] + r, size)
                if c["step"][1]:
                    cols = bass.ds(turn.i * c["step"][1] + col, c["n"])
            if c["cols2"]:
                n1, col2 = c["cols2"]
                return [((0, n1), w[0, rows, col:col + n1], "c"), ((n1, c["n"]), w[0, rows, col2:col2 + c["n"] - n1], "c")]
            return [((0, c["n"]), w[0, rows, cols], "c")]

        def rest(engine, g):
            s, w = g % RING, groups[g]["width"]
            return engine.tensor_tensor(wlo[:, s, 0:w], raw[:, s, 0:w], whi[:, s, 0:w].bitcast(F32), ALU.subtract)

        def walk(eng, visit, name):
            for items, reps, per in segments:
                if reps == 1:
                    for kind, what in items:
                        visit(kind, what, Turn())
                else:
                    with eng.Fori(0, reps) as i:
                        turn = Turn(i, per)
                        for kind, what in items:
                            visit(kind, what, turn)

        block = ctx.enter_context(nc.Block())

        @block.sync
        def _(sp):
            for m in range(4):
                for t in range(NT):
                    sp.dma_start(xres[:, t, m * CH:(m + 1) * CH], a["x"][0, t * P:(t + 1) * P, m * CH:(m + 1) * CH]).then_inc(x_landed[m], 16)

            def visit(kind, what, turn):
                if kind == "G":
                    g, s = what["g"], what["g"] % RING
                    if g >= RING:
                        wait(sp, lo_ready[s], lo_count(g - RING), turn.lo[s])
                    c = what["chunk"]
                    for (lo, hi), src, mode in weights(c, what["i"], turn):
                        if mode == "l":
                            dst = raw[:, s, :].rearrange("p (l e) -> p l e", l=8)
                        else:
                            dst = raw[:, s, 0:c["gk"] * c["n"]].rearrange("p (k n) -> p k n", k=c["gk"])[:, :, lo:hi]
                            src = src.rearrange("(k p) n -> p k n", p=P)
                        sp.dma_start(dst, src).then_inc(w_landed[s], 16)
                elif kind == "load_mem":
                    j = what["after_j"]
                    wait(sp, aux_done, j + 1)
                    for t in range(NT):
                        sp.dma_start(val["mem"][:, t, :], a["mem"][0, t * P:(t + 1) * P, :]).then_inc(mem_landed, 16)
                elif kind == "load_gain":
                    sp.dma_start(gain_rows, a["g_final"].partition_broadcast(P)).then_inc(gain_landed, 16)
                elif kind == "store":
                    m = what["m"]
                    wait(sp, rows_ready, what["rows_r"])
                    for t in range(NT):
                        sp.dma_start(out[0, t * P:(t + 1) * P, m * CH:(m + 1) * CH], xres[:, t, m * CH:(m + 1) * CH]).then_inc(stored, 16)

            walk(sp, visit, "sp")
            sp.wait_ge(stored, 16 * NT * D // CH)

        @block.gpsimd
        def _(pool):
            n = [0]

            def step(ins):
                ins.then_inc(pool_step, 1)
                n[0] += 1
                pool.wait_ge(pool_step, n[0])

            step(nc.gpsimd.memset(ident[:, :], 0.0))
            nc.gpsimd.affine_select(out=ident[:, :], in_=ident[:, :], pattern=[[-1, P]], compare_op=ALU.not_equal, fill=1.0,
                                    base=0, channel_multiplier=1).then_inc(consts_ready, 1)
            step(nc.gpsimd.memset(causal[:, :], 0.0))
            for lo in (0, 2 * P):
                step(nc.gpsimd.affine_select(out=causal[:, lo:lo + P], in_=causal[:, lo:lo + P], pattern=[[-1, P]],
                                             compare_op=ALU.is_ge, fill=NEG, base=0, channel_multiplier=1))
            step(nc.gpsimd.memset(tri_ones[:, :], 1.0))
            step(nc.gpsimd.affine_select(out=tri_ones[:, 0:P], in_=tri_ones[:, 0:P], pattern=[[1, P]],
                                         compare_op=ALU.is_ge, fill=0.0, base=0, channel_multiplier=-1))
            freq = (np.float32(THETA) ** (-np.arange(ROPE_HALF, dtype=np.float32) * np.float32(2.0 / (2 * ROPE_HALF)))).astype(np.float32)
            for i in range(ROPE_HALF):
                ins = nc.gpsimd.memset(inv[:, i:i + 1], float(freq[i]))
            ins.then_inc(consts_ready, 1)

            def distances():
                step(nc.gpsimd.iota(iota_i[:, 0:P], pattern=[[-1, P]], base=0, channel_multiplier=1))
                step(nc.gpsimd.iota(iota_i[:, P:3 * P], pattern=[[-1, 2 * P]], base=P, channel_multiplier=1))
                step(nc.gpsimd.tensor_copy(dist, iota_i))
                for lo in (0, 2 * P):
                    step(nc.gpsimd.affine_select(out=dist[:, lo:lo + P], in_=dist[:, lo:lo + P], pattern=[[-1, P]],
                                                 compare_op=ALU.is_ge, fill=FAR, base=0, channel_multiplier=1))
                step(nc.gpsimd.iota(iota_i[:, 0:64], pattern=[[P, NT], [-CMP_STRIDE, 32]], base=-(CMP_LEN - 1), channel_multiplier=1))
                step(nc.gpsimd.memset(misc[:, 3 * P:5 * P], FAR))
                step(nc.gpsimd.memset(misc[:, 5 * P:7 * P], 0.0))
                for g in range(KV_HEADS):
                    d, s = dist_cmp[:, g, :, 32 * g:32 * g + 32], seen_cmp[:, g, :, 32 * g:32 * g + 32]
                    step(nc.gpsimd.tensor_copy(d, iota_i[:, 0:64].rearrange("p (t n) -> p t n", t=NT)))
                    step(nc.gpsimd.memset(s, 1.0))
                    for v, fill in ((d, FAR), (s, 0.0)):
                        ins = nc.gpsimd.affine_select(out=v, in_=v, pattern=[[P, NT], [-CMP_STRIDE, 32]], compare_op=ALU.is_ge,
                                                      fill=fill, base=-(CMP_LEN - 1), channel_multiplier=1)
                        if g == KV_HEADS - 1 and v is s:
                            ins.then_inc(alibi_ready, 1)
                        else:
                            step(ins)

            def visit(kind, what, turn):
                if kind == "G" and what["g"] % RING < RING - 1:
                    wait(pool, hi_ready, what["g"] + 1, turn.g)
                    rest(nc.gpsimd, what["g"]).then_inc(lo_pool, 1)
                elif kind == "load_gain":
                    distances()

            walk(pool, visit, "pool")

        @block.scalar
        def _(act_e):
            act_e.dma_start(g_rows[0:KT, :], a["g_mix"].rearrange("a (k p) -> (a k) p", p=P)).then_inc(gmix_landed, 16)
            n, rstds, xs = [0], [0], [0]

            def step(ins):
                ins.then_inc(act_step, 1)
                n[0] += 1
                act_e.wait_ge(act_step, n[0])

            def round_group(g, turn):
                s, w = g % RING, groups[g]["width"]
                wait(act_e, w_landed[s], groups[g]["landed"], turn.landed)
                if g >= RING:
                    wait(act_e, group_done, g - RING + 1, turn.g)
                nc.scalar.activation(whi[:, s, 0:w], raw[:, s, 0:w], ACT.Copy).then_inc(hi_ready, 1)

            loads = 0
            g_src = [("g_mem_q", KT), ("g_mem_kv", KT), ("g_ff", KT), ("attn_norm_2", KT), ("ffn_norm_2", KT), ("g_cq", 4),
                     ("fox_q_norm_2", 1), ("fox_k_norm_2", 1), ("nsa_q_norm_2", 1), ("cmp_k_norm_2", 1), ("slc_k_norm_2", 1), ("win_k_norm_2", 1), ("g_final", KT)]
            for name, rows in g_src:
                v = a[name].rearrange("(k p) -> k p", p=P) if name == "g_final" else a[name].rearrange("a (k p) -> (a k) p", p=P)
                act_e.dma_start(g_rows[G_ROWS[name]:G_ROWS[name] + rows, :], v).then_inc(small_landed, 16)
                loads += 1
            for i, name in enumerate(("cmp_pos_k_2", "cmp_pos_v_2")):
                act_e.dma_start(p_rows[32 * i:32 * i + 32, :], a[name][0]).then_inc(small_landed, 16)
                loads += 1
            act_e.dma_start(posi[:, :], a["positions"].rearrange("a (t p) -> p (a t)", p=P), allow_slow_non_contiguous=True).then_inc(small_landed, 16)
            act_e.dma_start(s_("bias"), a["fox_forget_bias_2"][0].partition_broadcast(P)).then_inc(small_landed, 16)
            assert loads + 2 == SMALL_LOADS
            for g in range(RING - 1):
                round_group(g, Turn())

            def leave(c, turn):
                ev = c["ev"]
                if ev not in ("gate", "silu"):
                    return
                wait(act_e, group_done, c["end"], turn.g)
                wait(act_e, rstd_ready, rstds[0])
                if ev == "silu" and c["c"] >= 2:
                    wait(act_e, chunk_out[(c["c"] + 1) % 2], (c["c"] + 1) // 2, turn.c2)
                for t in range(NT):
                    src = prod_bank[c["c"] % 2 * 2 + t][:, :]
                    if ev == "gate":
                        ins = nc.scalar.activation(val[c["to"]][:, t, c["off"]:c["off"] + CH], src, ACT.Tanh, scale=s_("half_h", t, t + 1))
                    else:
                        ins = nc.scalar.activation(stage[:, 0, t, :], src, ACT.Silu, scale=s_("rstd_h", t, t + 1))
                ins.then_inc(chunk_out[c["c"] % 2], 1)

            def visit(kind, what, turn):
                if kind == "G":
                    if what["g"] + RING - 1 < len(groups):
                        round_group(what["g"] + RING - 1, turn)
                elif kind == "E":
                    leave(what, turn)
                    if what["ev"] == "fg":
                        act_e.wait_ge(forget_in, 1)
                        step(nc.scalar.activation(s_("e16"), s_("e16"), ACT.Exp, scale=-1.0))
                        nc.scalar.activation(s_("e16"), s_("e16"), ACT.Ln, bias=1.0).then_inc(forget_act, 1)
                        nc.scalar.activation(s_("gate"), s_("gate"), ACT.Tanh, scale=0.5).then_inc(gate_act, 1)
                elif kind == "rope":
                    act_e.wait_ge(angle_ready, 1)
                    nc.scalar.activation(s_("sin_in"), s_("sin_in"), ACT.Sin)
                    nc.scalar.activation(s_("red"), s_("red"), ACT.Sin).then_inc(sine_ready, 1)
                elif kind == "rstd":
                    rstds[0] += 1
                elif kind == "X":
                    x, j = xs[0], what["j"]
                    xs[0] += 1
                    act_e.wait_ge(aux_done, j + 1)
                    if x >= 2:
                        act_e.wait_ge(scored, x - 1)
                    nc.scalar.activation(rel[:, x % 2, :], aux_bank[j % 2][:, :], ACT.Relu).then_inc(aux_out[j % 2], 1)
                elif kind == "S":
                    u = what["u"]
                    act_e.wait_ge(row_max_ready, u + 1)
                    for t, (lo, hi) in enumerate(spans(what)):
                        v = s_sb[:, u % 2, lo:hi]
                        src = s_bank[u % 2][:, lo:hi] if what["kind"] == "mem" else v
                        total = None if what["kind"] == "cmp" else s_("rsum", u % 2 * 2 + t, u % 2 * 2 + t + 1)
                        ins = nc.scalar.activation(v, src, ACT.Exp, bias=s_("nmax", u % 2 * 2 + t, u % 2 * 2 + t + 1), scale=1.0, accum_out=total)
                    ins.then_inc(exp_done, 1)

            walk(act_e, visit, "act")

        @block.tensor
        def _(pe):
            buf_j, val_c, pt_j, seen, mem_units = {}, {}, {}, set(), []

            def aux_wait(j):
                if j not in seen:
                    seen.add(j)
                    pe.wait_ge(aux_out[j % 2], j // 2 + 1)

            def group(what, turn):
                c, i, g = what["chunk"], what["i"], what["g"]
                s, par = g % RING, c["c"] % 2
                if i == 0 and c["c"] >= 2:
                    wait(pe, chunk_out[par], c["c"] // 2, turn.c2)
                for j in what["need_j"]:
                    wait(pe, aux_out[j % 2], j // 2 + 1, turn.j2)
                wait(pe, lo_ready[s], lo_count(g), turn.lo[s])
                hi, lo = act[c["src"]]
                if c["kind"] == "cmp":
                    if i == 0:
                        pe.wait_ge(blocks_ready, 1)
                    for l in range(8):
                        at_l = (c["k0"] * SEQ) + (8 * i + l) * 64
                        rhs_hi, rhs_lo = whi[:, s, l * P:(l + 1) * P], wlo[:, s, l * P:(l + 1) * P]
                        o = prod_bank[par * 2][:, 0:P]
                        first, last = i == 0 and l == 0, i == 3 and l == 7
                        pe.matmul(o, hi[:, at_l:at_l + P], rhs_hi, start=first, stop=False)
                        pe.matmul(o, hi[:, at_l:at_l + P], rhs_lo, start=False, stop=False)
                        ins = pe.matmul(o, lo[:, at_l:at_l + P], rhs_hi, start=False, stop=last)
                    ins.then_inc(group_done, 1)
                    return
                for kk in range(c["gk"]):
                    k = c["gk"] * i + kk
                    rhs_hi, rhs_lo = (w[:, s, kk * c["n"]:(kk + 1) * c["n"]] for w in (whi, wlo))
                    for t in range(NT):
                        cols = slice((c["k0"] + k) * SEQ + t * P, (c["k0"] + k) * SEQ + (t + 1) * P)
                        o = prod_bank[par * 2 + t][:, 0:c["n"]]
                        pe.matmul(o, hi[:, cols], rhs_hi, start=k == 0, stop=False)
                        pe.matmul(o, hi[:, cols], rhs_lo, start=False, stop=False)
                        ins = pe.matmul(o, lo[:, cols], rhs_hi, start=False, stop=k == c["kt"] - 1)
                ins.then_inc(group_done, 1)

            def visit(kind, what, turn):
                if kind == "init":
                    pe.wait_ge(consts_ready, 1)
                    return
                if kind == "G":
                    group(what, turn)
                    return
                if kind == "E" and what["ev"] in ("value", "kv", "cmpv"):
                    val_c[what.get("to", "vcmp")] = what["c"]
                if kind == "S":
                    u = what["u"]
                    if what["q"] in buf_j:
                        aux_wait(buf_j[what["q"]])
                    aux_wait(buf_j[what["kk"]])
                    if u >= 2:
                        pe.wait_ge(row_max_ready, u - 1)
                        if mem_units and mem_units[-1] >= u - 2:
                            pe.wait_ge(exp_done, u - 1)
                    if what["kind"] == "mem":
                        mem_units.append(u)
                    q, k = qk[what["q"]][:, what["h"], :], qk[what["kk"]][:, what["kh"], :]
                    for t, (lo, hi) in enumerate(spans(what)):
                        fox = what["kind"] == "fox"
                        o = s_bank[u % 2][:, lo:hi]
                        ins = pe.matmul(o, q[:, t * P:(t + 1) * P], k[:, 0:hi - lo], start=True, stop=not fox)
                        if fox:
                            aux_wait(buf_j["cum"])
                            h = what["h"]
                            ins = pe.matmul(o, ident[0:8, h:h + 1].broadcast_to([8, P]), cum_t[:, 0:hi - lo], start=False, stop=True)
                    ins.then_inc(scores_done, 1)
                    return
                if kind not in ("T", "P", "O", "X", "C", "V"):
                    return
                j = what["j"]
                b = aux_bank[j % 2]
                if j >= 2:
                    wait(pe, aux_out[j % 2], j // 2, turn.j2)
                if kind == "V":
                    first = what["which"] == 0
                    pe.wait_ge(gmix_landed if first else small_landed, 16 if first else 16 * SMALL_LOADS)
                    rows, src = ((KT, g_rows), (N_GROWS, g_rows), (64, p_rows))[what["which"]]
                    ins = pe.transpose(b[:, 0:rows], src[0:rows, :], ident[0:rows, 0:rows])
                elif kind == "T":
                    if "r_fixed" in what["rows"]:
                        pe.wait_ge(x_landed[what["col"] // CH] if what["src"] == "x" else mem_landed, 16 * NT)
                    elif what["rows_c"] is not None:
                        c = what["rows_c"]
                        wait(pe, chunk_out[c % 2], c // 2 + 1, turn.c2)
                    else:
                        wait(pe, rows_ready, what["rows_r"], turn.r)
                    if what["src"] == "kcmp":
                        ins = pe.transpose(b[:, 0:64], k_cmp, ident[0:64, 0:64])
                    else:
                        src = {"stage": lambda: stage[:, what["rows_s"] % 2], "prod": lambda: stage[:, 1]}.get(what["src"], lambda: val[what["src"]])()
                        for kk in range(1 if what.get("one") else 2):
                            for t in range(NT):
                                ins = pe.transpose(b[:, kk * SEQ + t * P:kk * SEQ + (t + 1) * P],
                                                   src[:, t, what["col"] + kk * P:what["col"] + (kk + 1) * P], ident[:, :])
                    if what["to"] not in "AB":
                        buf_j[what["to"]] = j
                elif kind == "X":
                    t, w = what["t"], P * (what["t"] + 1)
                    aux_wait(buf_j["qi"])
                    aux_wait(buf_j["kidx"])
                    for i, h in enumerate(what["heads"]):
                        r = slice(64 * (h % 2), 64 * (h % 2) + 64)
                        ins = pe.matmul(b[:, i * w:(i + 1) * w], qk["qi"][r, h // 2, t * P:(t + 1) * P], kidx[r, 0:w], start=True, stop=True)
                elif kind == "P":
                    u = what["unit"]["u"]
                    pe.wait_ge(probs_ready, u + 1)
                    v = s_sb[:, u % 2, :]
                    for lo, hi, to in transposed(what["unit"]):
                        ins = pe.transpose(b[0:hi - lo, to:to + P], v[:, lo:hi], ident[:, :])
                    pt_j[u] = j
                elif kind == "O":
                    for i, (unit, slot) in enumerate(zip(what["units"], what["slots"])):
                        aux_wait(pt_j[unit["u"]])
                        cc = val_c[unit["v"]]
                        if ("c", cc) not in seen:
                            seen.add(("c", cc))
                            pe.wait_ge(chunk_out[cc % 2], cc // 2 + 1)
                        last = i == len(what["units"]) - 1
                        if unit["kind"] == "cmp":
                            ins = pe.matmul(b[:, 0:SEQ], v_cmp, pt_of(unit, slot)[0:64, 0:SEQ], start=i == 0, stop=last)
                            continue
                        v, pt = val[unit["v"]], pt_of(unit, slot)
                        h = unit["kh"] * HD
                        pe.matmul(b[:, 0:SEQ], v[:, 0, h:h + HD], pt[:, 0:SEQ], start=i == 0, stop=False)
                        o, r = (b[:, 0:SEQ], pt[:, SEQ:2 * SEQ]) if unit["kind"] == "mem" else (b[:, P:SEQ], pt[:, SEQ:3 * P])
                        ins = pe.matmul(o, v[:, 1, h:h + HD], r, start=False, stop=last)
                elif kind == "C":
                    if what["which"] == 0:
                        wait(pe, rows_ready, what["rows_r"])
                        pe.matmul(b[0:8, 0:SEQ], s_("logf", 0, 8), tri_ones[:, :], start=True, stop=False)
                        ins = pe.matmul(b[0:8, P:SEQ], s_("logf", 8, 16), tri_ones[:, 0:P], start=False, stop=True)
                        buf_j["cum"] = j
                    else:
                        pe.matmul(b[:, 0:8], tri_ones[:, 0:P], s_("logf", 0, 8), start=True, stop=True)
                        pe.matmul(b[:, 8:16], tri_ones[:, P:2 * P], s_("logf", 0, 8), start=True, stop=False)
                        ins = pe.matmul(b[:, 8:16], tri_ones[:, 0:P], s_("logf", 8, 16), start=False, stop=True)
                ins.then_inc(aux_done, 1)

            walk(pe, visit, "pe")

        @block.vector
        def _(dve):
            n, base, xs = [0], [0], [0]
            v_e = nc.vector

            def step(ins):
                ins.then_inc(dve_step, 1)
                n[0] += 1
                dve.wait_ge(dve_step, base[0] + n[0])

            def rsqrt(to, ss, m, dim):
                ms, y, t1 = s_("ms", 0, m), s_("y", 0, m), s_("t1", 0, m)
                step(v_e.tensor_scalar(ms, ss, 1.0 / dim, EPS, ALU.mult, ALU.add))
                step(v_e.tensor_scalar(newton_i[:, 0:m], ms.bitcast(I32), 1, None, ALU.logical_shift_right))
                step(v_e.tensor_scalar(y.bitcast(I32), newton_i[:, 0:m], -1.0, float(0x5F3759DF), ALU.mult, ALU.add))
                for i in range(4):
                    step(v_e.tensor_tensor(t1, y, y, ALU.mult))
                    step(v_e.scalar_tensor_tensor(t1, t1, -0.5, ms, ALU.mult, ALU.mult))
                    step(v_e.scalar_tensor_tensor(to if i == 3 else y, t1, 1.5, y, ALU.add, ALU.mult))

            def squares(src, col, m):
                for t in range(NT):
                    ins = v_e.tensor_tensor_reduce(scratch[:, :], src[:, t, col:col + CH], src[:, t, col:col + CH], 1.0, 0.0,
                                                   ALU.mult, ALU.add, s_("ss", 4 * t + m, 4 * t + m + 1))
                    if t == 0:
                        step(ins)
                return ins

            def rope(v, heads, half, tr, last):
                tmp = scratch[:, 0:NT * heads * 2 * half].rearrange("p (t h d) -> p t h d", t=NT, h=heads)
                shape = [P, NT, heads, half]
                v_e.tensor_tensor(tmp[:, :, :, 0:half], v[:, :, :, half:2 * half], tr[:, 1, :, 0:half].unsqueeze(2).broadcast_to(shape), ALU.mult)
                step(v_e.tensor_tensor(tmp[:, :, :, half:], v[:, :, :, 0:half], tr[:, 1, :, half:2 * half].unsqueeze(2).broadcast_to(shape), ALU.mult))
                rot = v[:, :, :, 0:2 * half]
                step(v_e.tensor_tensor(rot, rot, tr[:, 0].unsqueeze(2).broadcast_to([P, NT, heads, 2 * half]), ALU.mult))
                ins = v_e.tensor_tensor(rot, rot, tmp, ALU.add)
                if last is None:
                    step(ins)
                else:
                    ins.then_inc(last, 1)

            def head_norm(s, heads):
                for t in range(NT):
                    sq = scratch[:, 0:heads * HD]
                    v = stage[:, s, t, 0:heads * HD]
                    step(v_e.tensor_tensor(sq, v, v, ALU.mult))
                    step(v_e.tensor_reduce(s_("hss", heads * t, heads * t + heads), sq.rearrange("p (h d) -> p h d", h=heads), AX.X, ALU.add))
                rsqrt(s_("hrstd", 0, NT * heads), s_("hss", 0, NT * heads), NT * heads, HD)
                v = stage[:, s, :, 0:heads * HD].rearrange("p t (h d) -> p t h d", h=heads)
                r = s_("hrstd", 0, NT * heads).rearrange("p (t h) -> p t h", t=NT).unsqueeze(3).broadcast_to([P, NT, heads, HD])
                v_e.tensor_tensor(v, v, r, ALU.mult).then_inc(rows_ready, 1)

            def rope_tables():
                dve.wait_ge(small_landed, 16 * SMALL_LOADS)
                dve.wait_ge(consts_ready, 2)
                step(v_e.tensor_copy(s_("posf"), posi[:, :]))
                ang, k, red, half_in = s_("ang"), s_("turns"), s_("red"), s_("sin_in")
                for t in range(NT):
                    ins = v_e.tensor_scalar(ang[:, 16 * t:16 * t + 16], inv[:, :], s_("posf", t, t + 1), None, ALU.mult)
                step(ins)
                step(v_e.tensor_scalar(k, ang, 1.0 / (2 * np.pi), MAGIC, ALU.mult, ALU.add))
                step(v_e.tensor_scalar(k, k, MAGIC, None, ALU.subtract))
                step(v_e.scalar_tensor_tensor(red, k, -TWO_PI[0], ang, ALU.mult, ALU.add))
                for part_of in TWO_PI[1:]:
                    step(v_e.scalar_tensor_tensor(red, k, -part_of, red, ALU.mult, ALU.add))
                step(v_e.tensor_scalar(red, red, PI_IN, -PI_IN, ALU.min, ALU.max))
                v_e.tensor_scalar(half_in, red, 0.5, None, ALU.mult).then_inc(angle_ready, 1)

            def rope_signs():
                dve.wait_ge(sine_ready, 1)
                sn = s_("red").rearrange("p (t i) -> p t i", t=NT)
                step(v_e.tensor_tensor(s_("ang"), s_("sin_in"), s_("sin_in"), ALU.mult))
                step(v_e.tensor_scalar(s_("ang"), s_("ang"), -2.0, 1.0, ALU.mult, ALU.add))
                cs = s_("ang").rearrange("p (t i) -> p t i", t=NT)
                for tr, half, st in ((trig, ROPE_HALF, 1), (trig8, ROPE_HALF // 2, 2)):
                    sv, cv = sn[:, :, 0:ROPE_HALF:st], cs[:, :, 0:ROPE_HALF:st]
                    v_e.tensor_copy(tr[:, 0, :, 0:half], cv)
                    v_e.tensor_copy(tr[:, 0, :, half:2 * half], cv)
                    v_e.tensor_scalar(tr[:, 1, :, 0:half], sv, -1.0, None, ALU.mult)
                    ins = v_e.tensor_copy(tr[:, 1, :, half:2 * half], sv)
                step(ins)

            def leave(c, turn):
                ev, par = c["ev"], c["c"] % 2
                out_sem, out_n = chunk_out[par], c["c"] // 2 + 1
                b = [prod_bank[par * 2 + t][:, 0:c["n"]] for t in range(NT)]
                r = [s_("rstd_" + c["rstd"], t, t + 1) for t in range(NT)] if "rstd" in c else None
                if ev == "silu":
                    return
                if ev == "gate":
                    wait(dve, out_sem, out_n)
                    v = val[c["to"]][:, :, c["off"]:c["off"] + CH]
                    step(v_e.tensor_scalar(v, v, 0.5, 0.5, ALU.mult, ALU.add))
                    return
                wait(dve, group_done, c["end"], turn.g)
                s = c["s"] % 2 if "s" in c else None

                def scaled(dst, lo, hi, final=True):
                    for t in range(NT):
                        ins = v_e.tensor_scalar(dst[t], b[t][:, lo:hi], r[t], None, ALU.mult)
                    if final:
                        ins.then_inc(out_sem, 1)

                if ev in ("cq", "rope", "ropei", "idx", "plain", "hnorm"):
                    scaled([stage[:, s, t, 0:c["n"]] for t in range(NT)], 0, c["n"])
                    if ev != "plain":
                        wait(dve, out_sem, out_n)
                    if ev == "cq":
                        for t in range(NT):
                            v = stage[:, s, t, :]
                            ins = v_e.tensor_tensor_reduce(scratch[:, :], v, v, 1.0, 0.0, ALU.mult, ALU.add, s_("ss_cq", t, t + 1))
                            if t == 0:
                                step(ins)
                        ins.then_inc(rows_ready, 1)
                        dve.wait_ge(rows_ready, c["r"])
                        rsqrt(s_("rstd_cq"), s_("ss_cq"), NT, CH)
                    elif ev == "rope":
                        rope(stage[:, s].rearrange("p t (h d) -> p t h d", h=4), 4, ROPE_HALF, trig, rows_ready)
                    elif ev == "ropei":
                        rope(stage[:, s].rearrange("p t (h d) -> p t h d", h=8), 8, ROPE_HALF // 2, trig8, rows_ready)
                    elif ev == "idx":
                        w = s_("w_idx").rearrange("p (t h) -> p t h", t=NT)
                        step(v_e.tensor_scalar(w, stage[:, s, :, IDX_D:IDX_D + IDX_H], W_IDX_SCALE, None, ALU.mult))
                        rope(stage[:, s, :, 0:IDX_D].unsqueeze(2), 1, ROPE_HALF // 2, trig8, None)
                        v_e.tensor_copy(stage[:, s, :, IDX_D:2 * IDX_D], stage[:, s, :, 0:IDX_D]).then_inc(rows_ready, 1)
                    elif ev == "hnorm":
                        head_norm(s, c["heads"])
                elif ev == "value":
                    scaled([val[c["to"]][:, t, c["off"]:c["off"] + CH] for t in range(NT)], 0, CH)
                elif ev == "kv":
                    scaled([stage[:, s, t, 0:2 * HD] for t in range(NT)], 0, 2 * HD, final=False)
                    scaled([val[c["to"]][:, t, :] for t in range(NT)], 2 * HD, 4 * HD)
                    wait(dve, out_sem, out_n)
                    head_norm(s, 2)
                elif ev == "ya":
                    for t in range(NT):
                        g = val["sa"][:, t, c["off"]:c["off"] + CH]
                        ins = v_e.tensor_tensor(g, b[t], g, ALU.mult)
                    ins.then_inc(out_sem, 1)
                elif ev == "yb":
                    for t in range(NT):
                        g = val["sb"][:, t, c["off"]:c["off"] + CH]
                        ins = v_e.tensor_tensor(g, b[t], g, ALU.mult)
                    ins.then_inc(out_sem, 1)
                    wait(dve, out_sem, out_n)
                    ga, gb = (val[x][:, :, c["off"]:c["off"] + CH] for x in ("sa", "sb"))
                    v_e.tensor_tensor(ga, ga, gb, ALU.add).then_inc(rows_ready, 1)
                elif ev == "addx":
                    for t in range(NT):
                        x = xres[:, t, c["off"]:c["off"] + CH]
                        ins = v_e.tensor_tensor(x, b[t], x, ALU.add)
                    ins.then_inc(out_sem, 1)
                    if c["rows"]:
                        wait(dve, out_sem, out_n, turn.c2)
                        squares(xres, c["off"], c["off"] // CH).then_inc(rows_ready, 1)
                        wait(dve, rows_ready, c["r"], turn.r)
                        if c.get("twice"):
                            m = c["off"] // CH
                            dve.wait_ge(gain_landed, 16)
                            for t in range(NT):
                                step(v_e.tensor_tensor(scratch[:, :], xres[:, t, c["off"]:c["off"] + CH], gain_rows[:, c["off"]:c["off"] + CH], ALU.mult))
                                step(v_e.tensor_tensor_reduce(scratch[:, :], scratch[:, :], scratch[:, :], 1.0, 0.0, ALU.mult, ALU.add,
                                                              s_("ss2", 4 * t + m, 4 * t + m + 1)))
                elif ev == "relu2":
                    for t in range(NT):
                        ins = v_e.tensor_scalar(stage[:, s, t, :], b[t], r[t], 0.0, ALU.mult, ALU.max)
                    ins.then_inc(out_sem, 1)
                    wait(dve, out_sem, out_n, turn.c2)
                    v_e.tensor_tensor(stage[:, s], stage[:, s], stage[:, s], ALU.mult).then_inc(rows_ready, 1)
                elif ev == "glu":
                    wait(dve, chunk_out[(c["c"] + 1) % 2], (c["c"] + 1) // 2, turn.c2)
                    for t in range(NT):
                        ins = v_e.scalar_tensor_tensor(stage[:, 1, t, :], b[t], r[t], stage[:, 0, t, :], ALU.mult, ALU.mult)
                    ins.then_inc(out_sem, 1)
                elif ev == "cmpk":
                    step(v_e.tensor_copy(k_cmp, prod_bank[par * 2][0:64, 0:P]))
                    ss = s_("hss", 0, 1)[0:64]
                    v_e.tensor_tensor_reduce(cmp_junk, k_cmp, k_cmp, 1.0, 0.0, ALU.mult, ALU.add, ss).then_inc(out_sem, 1)
                    wait(dve, out_sem, out_n)
                    rsqrt(s_("hrstd", 0, 1), s_("hss", 0, 1), 1, HD)
                    v_e.tensor_scalar(k_cmp, k_cmp, s_("hrstd", 0, 1)[0:64], None, ALU.mult).then_inc(rows_ready, 1)
                elif ev == "cmpv":
                    v_e.tensor_copy(v_cmp, prod_bank[par * 2][0:64, 0:P]).then_inc(out_sem, 1)
                elif ev == "fg":
                    z, gt = s_("logit"), s_("gate")
                    for t in range(NT):
                        v_e.tensor_scalar(gt[:, 24 * t:24 * t + 24], b[t][:, 8:32], r[t], None, ALU.mult)
                        ins = v_e.scalar_tensor_tensor(z[:, 8 * t:8 * t + 8], b[t][:, 0:8], r[t], s_("bias"), ALU.mult, ALU.add)
                    ins.then_inc(out_sem, 1)
                    wait(dve, out_sem, out_n)
                    v_e.scalar_tensor_tensor(s_("e16"), z, -1.0, z, ALU.mult, ALU.max).then_inc(forget_in, 1)
                    dve.wait_ge(forget_act, 1)
                    v_e.scalar_tensor_tensor(s_("logf"), z, 0.0, s_("e16"), ALU.min, ALU.subtract).then_inc(rows_ready, 1)
                    dve.wait_ge(gate_act, 1)
                    step(v_e.tensor_scalar(gt, gt, 0.5, 0.5, ALU.mult, ALU.add))

            def turned(what, turn):
                j, k = what["j"], what["k"]
                b, done = aux_bank[j % 2], aux_out[j % 2]
                if what["to"] in "AB":
                    hi, lo = act[what["to"]]
                    cols = slice(k * SEQ, (k + 2) * SEQ)
                    if "gain" not in what:
                        step(v_e.tensor_copy(hi[:, cols], b[:, :]))
                        v_e.tensor_tensor(lo[:, cols], b[:, :], hi[:, cols].bitcast(F32), ALU.subtract).then_inc(done, 1)
                        return
                    g0 = G_ROWS[what["gain"]] + (what["gain_k"] + what["col"] // P if "gain_k" in what else k)
                    for kk in range(2):
                        c1 = slice((k + kk) * SEQ, (k + kk + 1) * SEQ)
                        ins = v_e.tensor_scalar(hi[:, c1], b[:, kk * SEQ:(kk + 1) * SEQ], gains[:, g0 + kk:g0 + kk + 1], None, ALU.mult)
                    step(ins)
                    for kk in range(2):
                        c1 = slice((k + kk) * SEQ, (k + kk + 1) * SEQ)
                        ins = v_e.scalar_tensor_tensor(lo[:, c1], b[:, kk * SEQ:(kk + 1) * SEQ], gains[:, g0 + kk:g0 + kk + 1],
                                                       hi[:, c1].bitcast(F32), ALU.mult, ALU.subtract)
                    ins.then_inc(done, 1)
                    return
                scale = what.get("scale") or 1.0
                if what["src"] == "kcmp":
                    g = G_ROWS["cmp_k_norm_2"]
                    v_e.tensor_scalar(qk["kcmp"][:, 0, :], b[:, 0:64], gains[:, g:g + 1], None, ALU.mult).then_inc(done, 1)
                    return
                if what["to"] == "kidx":
                    v_e.tensor_copy(kidx, b[:, 0:SEQ]).then_inc(done, 1)
                    return
                dst = qk[what["to"]][:, k:k + 2, :]
                src = b[:, :].rearrange("p (h t) -> p h t", h=2)
                if what.get("hgain"):
                    g = G_ROWS[what["hgain"]]
                    v_e.tensor_scalar(dst, src, gains[:, g:g + 1], scale, ALU.mult, ALU.mult).then_inc(done, 1)
                else:
                    v_e.tensor_scalar(dst, src, scale, None, ALU.mult).then_inc(done, 1)

            def biased(what):
                u, kind, h = what["u"], what["kind"], what["h"]
                b, v = s_bank[u % 2], s_sb[:, u % 2, :]
                dve.wait_ge(scores_done, u + 1)
                if kind == "dsa":
                    step(v_e.tensor_tensor(v[:, 0:3 * P], b[:, 0:3 * P], picked, ALU.add))
                elif kind == "moba":
                    step(v_e.tensor_tensor(v[:, 0:3 * P], b[:, 0:3 * P], causal[:, :], ALU.add))
                elif kind == "mem":
                    v = b
                elif kind == "alibi":
                    step(v_e.scalar_tensor_tensor(v[:, 0:3 * P], dist, -SLOPES[h], b[:, 0:3 * P], ALU.mult, ALU.add))
                elif kind == "cmp":
                    d = dist_cmp[:, what["g"]].rearrange("p t n -> p (t n)")
                    step(v_e.scalar_tensor_tensor(v[:, 0:P], d, -SLOPES[h], b[:, 0:P], ALU.mult, ALU.add))
                elif kind == "fox":
                    for t, (lo, hi) in enumerate(spans(what)):
                        ins = v_e.scalar_tensor_tensor(v[:, lo:hi], b[:, lo:hi], s_("cum_q", 8 * t + h, 8 * t + h + 1), causal[:, lo:hi],
                                                       ALU.add, ALU.add)
                    step(ins)
                for t, (lo, hi) in enumerate(spans(what)):
                    i = u % 2 * 2 + t
                    ins = v_e.tensor_reduce(s_("nmax", i, i + 1), v[:, lo:hi], AX.X, ALU.max, negate=True)
                ins.then_inc(row_max_ready, 1)

            def normalised(what):
                u, i = what["u"], what["u"] % 2 * 2
                v = s_sb[:, u % 2, :]
                rs, ri = s_("rsum", i, i + 2), s_("rinv", i, i + 2)
                dve.wait_ge(exp_done, u + 1)
                if what["kind"] == "cmp":
                    for t, (lo, hi) in enumerate(spans(what)):
                        ins = v_e.tensor_tensor_reduce(v[:, lo:hi], v[:, lo:hi], seen_cmp[:, what["g"], t], 1.0, 0.0, ALU.mult, ALU.add,
                                                       s_("rsum", i + t, i + t + 1))
                    step(ins)
                    step(v_e.tensor_scalar(rs, rs, 1e-30, None, ALU.max))
                step(v_e.reciprocal(ri, rs))
                if what["kind"] in ("cmp", "alibi"):
                    g = s_("gate").rearrange("p (t x) -> p t x", t=NT)[:, :, 3 * what["h"] + what["b"]]
                    step(v_e.tensor_tensor(ri, ri, g, ALU.mult))
                for t, (lo, hi) in enumerate(spans(what)):
                    ins = v_e.tensor_scalar(v[:, lo:hi], v[:, lo:hi], s_("rinv", i + t, i + t + 1), None, ALU.mult)
                ins.then_inc(probs_ready, 1)

            def blocks(what):
                src = qk[what["of"]]
                k, e0 = what["k"], 0 if what["of"] == "kc" else 32
                wait(dve, aux_out[0], 0)
                step(v_e.memset(blk_sum, 0.0))
                to = blk_sum.rearrange("p (l g n) -> p l g n", l=CMP_LEN, g=KV_HEADS)[:, :, :, 0:CMP_N]
                for half in range(2):
                    w = src[:, :, half * CMP_STRIDE:half * CMP_STRIDE + CMP_N * CMP_STRIDE].rearrange("p g (n l) -> p l g n", l=CMP_STRIDE)
                    ls = slice(half * CMP_STRIDE, (half + 1) * CMP_STRIDE)
                    for g in range(KV_HEADS):
                        e = pos_emb[:, e0 + half * CMP_STRIDE:e0 + (half + 1) * CMP_STRIDE].unsqueeze(2).broadcast_to([P, CMP_STRIDE, CMP_N])
                        ins = v_e.tensor_tensor(to[:, ls, g], w[:, :, g], e, ALU.add)
                step(ins)
                hi, lo = act["B"]
                cols = slice(k * SEQ, (k + 8) * SEQ)
                step(v_e.tensor_copy(hi[:, cols], blk_sum))
                step(v_e.tensor_tensor(lo[:, cols], blk_sum, hi[:, cols].bitcast(F32), ALU.subtract))
                if what["of"] == "vc":
                    for x in (hi, lo):
                        ins = v_e.memset(x[:, KT * SEQ:KT * SEQ + 64].bitcast(F32), 0.0)
                    ins.then_inc(blocks_ready, 1)

            def visit(kind, what, turn):
                if kind == "G":
                    g = what["g"] + 2
                    if g % RING == RING - 1 and g < len(groups):
                        wait(dve, hi_ready, g + 1, turn.g)
                        rest(v_e, g).then_inc(lo_dve, 1)
                elif kind == "rope":
                    rope_tables()
                    rope_signs()
                elif kind == "V":
                    dve.wait_ge(aux_done, what["j"] + 1)
                    lo, hi, dst = ((0, KT, gains), (KT, N_GROWS, gains), (0, 64, pos_emb))[what["which"]]
                    v_e.tensor_copy(dst[:, lo:hi], aux_bank[what["j"] % 2][:, lo:hi]).then_inc(aux_out[what["j"] % 2], 1)
                    dve.wait_ge(aux_out[what["j"] % 2], what["j"] // 2 + 1)
                    if what["which"] == 1:
                        ga, gf = (gains[:, G_ROWS[x]:G_ROWS[x] + KT] for x in ("attn_norm_2", "g_final"))
                        step(v_e.tensor_tensor(ga, ga, gf, ALU.mult))
                elif kind == "T":
                    wait(dve, aux_done, what["j"] + 1, turn.j2 * 2)
                    turned(what, turn)
                elif kind == "P":
                    dve.wait_ge(aux_done, what["j"] + 1)
                    unit, b = what["unit"], aux_bank[what["j"] % 2]
                    m, w = {"cmp": (64, SEQ), "mem": (P, 2 * SEQ)}.get(unit["kind"], (P, 3 * P))
                    v_e.tensor_copy(pt_of(unit, what["slot"])[0:m, 0:w], b[0:m, 0:w]).then_inc(aux_out[what["j"] % 2], 1)
                elif kind == "O":
                    dve.wait_ge(aux_done, what["j"] + 1)
                    b = aux_bank[what["j"] % 2][:, 0:SEQ]
                    hi, lo = (x[:, what["k"] * SEQ:(what["k"] + 1) * SEQ] for x in act["B"])
                    step(v_e.tensor_copy(hi, b))
                    v_e.tensor_tensor(lo, b, hi.bitcast(F32), ALU.subtract).then_inc(aux_out[what["j"] % 2], 1)
                elif kind == "C":
                    dve.wait_ge(aux_done, what["j"] + 1)
                    b, done = aux_bank[what["j"] % 2], aux_out[what["j"] % 2]
                    if what["which"] == 0:
                        v_e.tensor_scalar(cum_t[:, :], b[0:8, 0:SEQ], -1.0, None, ALU.mult).then_inc(done, 1)
                    else:
                        v_e.tensor_copy(s_("cum_q"), b[:, 0:16]).then_inc(done, 1)
                        dve.wait_ge(done, what["j"] // 2 + 1)
                elif kind == "X":
                    t, x, w = what["t"], xs[0], P * (what["t"] + 1)
                    xs[0] += 1
                    dve.wait_ge(aux_out[what["j"] % 2], what["j"] // 2 + 1)
                    sc = score[:, 0:P] if t == 0 else score[:, P:3 * P]
                    for i, h in enumerate(what["heads"]):
                        r, wh = rel[:, x % 2, i * w:(i + 1) * w], s_("w_idx", 16 * t + h, 16 * t + h + 1)
                        ins = v_e.tensor_scalar(sc, r, wh, None, ALU.mult) if h == 0 else \
                            v_e.scalar_tensor_tensor(sc, r, wh, sc, ALU.mult, ALU.add)
                        if i < len(what["heads"]) - 1:
                            step(ins)
                    ins.then_inc(scored, 1)
                    dve.wait_ge(scored, x + 1)
                elif kind == "K":
                    cols = slice(0, P) if what["t"] == 0 else slice(P, 3 * P)
                    sc, top = score[:, cols], s_("top")
                    if what["part"] == 0:
                        step(v_e.tensor_tensor(sc, sc, causal[:, cols], ALU.add))
                    for _ in range(TOPK // 8 // 4):
                        step(v_e.max(top, sc))
                        step(v_e.match_replace(sc, top, sc, TAKEN))
                    if what["part"] == 3:
                        step(v_e.tensor_scalar(picked[:, cols], sc, TAKEN, NEG, ALU.not_equal, ALU.mult))
                        step(v_e.tensor_tensor(picked[:, cols], picked[:, cols], causal[:, cols], ALU.add))
                elif kind == "E":
                    leave(what, turn)
                elif kind == "rstd":
                    of, name = what["of"], what["name"]
                    if of == "mem":
                        dve.wait_ge(mem_landed, 16 * NT)
                    if of == "mem" or what.get("first"):
                        for m in range(4):
                            if of == "x":
                                dve.wait_ge(x_landed[m], 16 * NT)
                            step(squares(val[of], m * CH, m))
                    ss = s_("ss2" if of == "x2" else "ss")
                    step(v_e.tensor_reduce(s_("rm", 0, 2), ss.rearrange("p (t m) -> p t m", t=NT), AX.X, ALU.add))
                    if of == "x2":
                        for _ in range(2):
                            step(v_e.tensor_tensor(s_("rm", 0, 2), s_("rm", 0, 2), s_("rstd_f"), ALU.mult))
                    rsqrt(s_("rstd_" + name), s_("rm", 0, 2), NT, D)
                    if of == "x2":
                        step(v_e.tensor_tensor(s_("rstd_h"), s_("rstd_h"), s_("rstd_f"), ALU.mult))
                    if name == "h":
                        v_e.tensor_scalar(s_("half_h"), s_("rstd_h"), 0.5, None, ALU.mult).then_inc(rstd_ready, 1)
                    else:
                        v_e.memset(s_("t1", 0, 1), 0.0).then_inc(rstd_ready, 1)
                elif kind == "renorm":
                    m = what["m"]
                    for t in range(NT):
                        x = xres[:, t, m * CH:(m + 1) * CH]
                        ins = v_e.scalar_tensor_tensor(x, x, s_("rstd_f", t, t + 1), gain_rows[:, m * CH:(m + 1) * CH], ALU.mult, ALU.mult)
                    step(ins)
                elif kind == "blocks":
                    blocks(what)
                elif kind == "S":
                    if what["kind"] == "cmp" and what["u"] == 20:
                        dve.wait_ge(alibi_ready, 1)
                    biased(what)
                elif kind == "N":
                    normalised(what)

            for items, reps, per in segments:
                if reps == 1:
                    for kind, what in items:
                        visit(kind, what, Turn())
                else:
                    chained = sum(kind == "T" for kind, _ in items)
                    start = n[0]
                    with dve.Fori(0, reps) as i:
                        base[0] = i * chained
                        for kind, what in items:
                            visit(kind, what, Turn(i, per))
                    assert n[0] - start == chained
                    n[0] += chained * (reps - 1)
                    base[0] = 0


SMALL_LOADS = 17


def spans(unit):
    if unit["kind"] == "cmp":
        return [(0, 64), (64, 128)]
    return [(0, SEQ), (SEQ, 2 * SEQ)] if unit["kind"] == "mem" else [(0, P), (P, 3 * P)]


def transposed(unit):
    if unit["kind"] == "cmp":
        return [(0, 64, 0), (64, 128, P)]
    if unit["kind"] == "mem":
        return [(0, P, 0), (2 * P, 3 * P, P), (P, 2 * P, 2 * P), (3 * P, 4 * P, 3 * P)]
    return [(0, P, 0), (P, 2 * P, P), (2 * P, 3 * P, 2 * P)]


_INS = ["x", "mem", "positions", "g_mix", "w_in", "g_cq", "w_uq", "w_iq", "w_dsa_o", "w_moba_o", "w_out", "g_mem_q", "g_mem_kv",
        "w_mem_q", "w_mem_kv", "w_mem_o", "g_ff", "w_ff1", "w_ff2", "g_final", "attn_norm_2", "w_in_2", "fox_forget_bias_2",
        "fox_q_norm_2", "fox_k_norm_2", "nsa_q_norm_2", "cmp_k_norm_2", "slc_k_norm_2", "win_k_norm_2", "cmp_pos_k_2", "cmp_pos_v_2",
        "cmp_w_k_2", "cmp_w_v_2", "w_out_2", "ffn_norm_2", "w_gate_2", "w_up_2", "w_down_2"]


def kernel(**inputs):
    import concourse.bacc as bacc
    from concourse.bass_utils import run_bass_kernel_spmd

    nc = bacc.Bacc("TRN2", target_bir_lowering=False, num_devices=1)
    arrays, aps = {}, {}
    for name in _INS:
        v = np.ascontiguousarray(inputs[name])
        arrays["in_" + name] = v
        aps[name] = nc.dram_tensor("in_" + name, v.shape, mybir.dt.from_np(v.dtype), kind="ExternalInput").ap()
    out = nc.dram_tensor("out_y", (1, SEQ, D), F32, kind="ExternalOutput").ap()
    two_blocks(nc, aps, out)
    r = run_bass_kernel_spmd(nc, [arrays], core_ids=[0])
    return r.results[0]["out_y"]
```

```python
from contextlib import ExitStack

import numpy as np

import concourse.bass as bass
from concourse import mybir

F32 = mybir.dt.float32
F32R = mybir.dt.float32r
I32 = mybir.dt.int32
ALU = mybir.AluOpType
ACT = mybir.ActivationFunctionType
AX = mybir.AxisListType

P = 128
SEQ = 256
NT = SEQ // P
D = 2048
KT = D // P
CH = 512
HD = 128
EPS = 1e-6
NEG = -1e30
FAR = 1e33
TAKEN = -3.0e38
SCALE = HD ** -0.5
TOPK = min(256, SEQ // 4)
IDX_H, IDX_D = 16, 64
W_IDX_SCALE = IDX_H ** -0.5 * IDX_D ** -0.5
ROPE_HALF = 16
THETA = 500000.0
FF = 8192
FF2 = 5632
RING = 4
GROUP = 2 * CH
CMP_N, CMP_STRIDE, CMP_LEN = 15, 16, 32
NSA_HEADS, KV_HEADS = 8, 2
SLOPES = [2.0 ** (-8.0 * (h + 1) / NSA_HEADS) for h in range(NSA_HEADS)]
MAGIC = 12582912.0
TWO_PI = (6.28125, float(np.float32(2 * np.pi - 6.28125) - np.float32(2 * np.pi - 6.28125) % np.float32(2.0 ** -20)))
TWO_PI = TWO_PI + (2 * np.pi - TWO_PI[0] - TWO_PI[1],)
PI_IN = 3.1415925

CQ, KA, VA, KIDX, QB, KB, VB, GLA, GLB = 0, 512, 1536, 2560, 2640, 3664, 4688, 5712, 7760
QF, KF, VF, FG, QN, KC, KS, KW, GT = 0, 1024, 2048, 3072, 3080, 4104, 4616, 5128, 5640

NSA_SHARES = (6, 13, 12, 9, 9, 9)

VA_PART, VF_PART = 368, 352

G_ROWS = {"g_mix": 0, "g_mem_q": 16, "g_mem_kv": 32, "g_ff": 48, "attn_norm_2": 64, "ffn_norm_2": 80,
          "g_cq": 96, "fox_q_norm_2": 100, "fox_k_norm_2": 101, "nsa_q_norm_2": 102, "cmp_k_norm_2": 103,
          "slc_k_norm_2": 104, "win_k_norm_2": 105, "g_final": 106}
N_GROWS = 122


def gemm(w, row0, col0, kt, src, k0=0, width=CH, need=(), rows=False, step=(0, 0), cols2=None, kind="gemm", gk=2, **more):
    return dict(w=w, row0=row0, col0=col0, kt=kt, src=src, k0=k0, n=width, need=need, rows=rows, step=step,
                cols2=cols2, kind=kind, gk=gk, count=8 if kind == "cmp" else kt // gk, **more)


def groups_of(c):
    return [("G", dict(chunk=c, i=i)) for i in range(c["count"])]


def weave(c, side=(), start=1):
    main, side = groups_of(c), list(side)
    slots = len(main) - start + 1
    out, done = [], 0
    for i, item in enumerate(main):
        out.append(item)
        if i + 1 >= start:
            want = -(-len(side) * (i + 2 - start) // slots)
            out += side[done:want]
            done = want
    out += side[done:] + [("E", c)]
    return [x for item in out for x in (item if isinstance(item, list) else [item])]


def lead(c, steps, ahead=2):
    out = list(steps[:ahead])
    for i, item in enumerate(groups_of(c)):
        out += [item] + list(steps[ahead + i:ahead + i + 1])
    return out + [("E", c)]


def alternate(c1, c2):
    one, two = groups_of(c1), groups_of(c2)
    return one[:2] + [x for pair in zip(one[2:], two) for x in pair] + [("E", c1)] + two[-2:] + [("E", c2)]


def squares(m, c=None, of="x"):
    return ("Q", dict(of=of, m=m, rows=c or dict(r_fixed=0)))


def turn(src, col, to, k, rows, **more):
    return ("T", dict(src=src, col=col, to=to, k=k, rows=rows, **more))


def turns(c, to, k, **more):
    return [turn("stage", 2 * i * P, to, k + 2 * i, c, **more) for i in range(2)]


def filled(steps):
    return [(what["k"], what) for _, what in steps]


def attention(units):
    out, m, values = [], len(units), []
    for i in range(m + 2):
        one, two = [], []
        if 1 <= i <= m:
            one.append(("N", units[i - 1]))
            two.append(("P", dict(unit=units[i - 1], slot=(i - 1) % 3)))
        if i < m:
            one.append(("S", units[i]))
        if i >= 2:
            values.append(("O", dict(units=[units[i - 2]], slots=[(i - 2) % 3], k=units[i - 2]["k"])))
            two.append(values[-1])
        out += [x for x in (one, two) if x]
    return out, values


def nsa_attention(units):
    out, m, values = [], len(units), []
    for i in range(m + 1):
        one, two = [], []
        if i >= 1:
            one.append(("N", units[i - 1]))
            two.append(("P", dict(unit=units[i - 1], slot=(i - 1) % 3)))
        if i < m:
            one.append(("S", units[i]))
        if i % 3 == 1 and i > 1:
            values.append(("O", dict(units=units[i - 4:i - 1], slots=[0, 1, 2], k=8 + i // 3 - 1)))
            two.insert(0, values[-1])
        out += [x for x in (one, two) if x]
    values.append(("O", dict(units=units[m - 3:m], slots=[0, 1, 2], k=8 + m // 3 - 1)))
    out.append([values[-1]])
    return out, values


def cut(steps, n, weights=None):
    weights = weights or [1] * n
    ends = [sum(weights[:i]) * len(steps) // sum(weights) for i in range(n + 1)]
    return [steps[a:b] for a, b in zip(ends, ends[1:])]


def plan():
    rows_x = dict(r_fixed=0)

    xt = [turn("x", 2 * i * P, "A", 2 * i, rows_x, gain="g_mix") for i in range(8)]
    seq = [("init", {}), ("V", dict(which=0))]

    def w_in(col, ev, **more):
        return gemm("w_in", 0, col, KT, "A", ev=ev, rstd="h", **more)

    cq = gemm("w_in", 0, CQ, KT, "A", need=filled(xt), ev="cq", rstd="h", rows=True)
    first = lead(cq, xt)
    for m in range(4):
        first.insert(first.index(xt[2 * m + 1]) + 1, squares(m))
    seq += first[:-1] + [("rstd", dict(of="x", name="h")), first[-1]]
    cqt = turns(cq, "B", 12, gain="g_cq", gain_k=0)
    ka0 = w_in(KA, "rope", rows=True)
    seq += weave(ka0, [("V", dict(which=1)), ("V", dict(which=2)), ("rope", {})], 2)
    ka1 = w_in(KA + CH, "rope", rows=True)
    seq += weave(ka1, cqt + turns(ka0, "ka", 0), 3)
    va_cut = [0, VA_PART, 2 * VA_PART]
    va = [w_in(VA + off, "value", width=VA_PART, to="va", off=off) for off in va_cut[:2]]
    idx = w_in(VA + va_cut[2], "idx", width=KIDX + 80 - VA - va_cut[2], off=va_cut[2], rows=True)
    seq += weave(idx, turns(ka1, "ka", 4), 3)
    seq += weave(va[0], [turn("stage", 0, "kidx", 0, idx, one=True)], 4) + weave(va[1])
    qi = [gemm("w_iq", 0, i * CH, 4, "B", 12, need=[(k - 12, t) for k, t in filled(cqt)] if i == 0 else (),
               ev="ropei", rstd="cq", rows=True) for i in range(2)]
    kb = [w_in(KB + i * CH, "rope", rows=True) for i in range(2)]
    seq += weave(qi[0]) + weave(qi[1])
    seq += weave(kb[0], turns(qi[0], "qi", 0) + turns(qi[1], "qi", 4), 2)
    index = [("X", dict(t=0, heads=[h0, h0 + 2, h0 + 4, h0 + 6])) for h0 in (0, 1, 8, 9)]
    index += [("X", dict(t=1, heads=[h0, h0 + 2])) for h0 in (0, 1, 4, 5, 8, 9, 12, 13)] 
    index += [("K", dict(t=t, part=i)) for t in range(NT) for i in range(4)]
    seq += weave(kb[1], turns(kb[0], "kb", 0) + index[:10], 2)
    qa = [gemm("w_uq", 0, i * CH, 4, "B", 12, ev="rope", rstd="cq", rows=True) for i in range(2)]
    vb = [w_in(VB + i * CH, "value", to="vb", off=i * CH) for i in range(2)]
    seq += weave(qa[0])
    seq += weave(vb[0], turns(kb[1], "kb", 4) + turns(qa[0], "qa", 0, scale=SCALE) + index[10:16], 2)
    seq += weave(qa[1])
    seq += weave(vb[1], index[16:18] + turns(qa[1], "qa", 4, scale=SCALE) + index[18:], 2)
    dsa = [dict(kind="dsa", q="qa", kk="ka", v="va", h=h, kh=h, k=h) for h in range(8)]
    steps, o_dsa = attention(dsa)
    part = cut(steps, 2)
    qb = [w_in(QB + i * CH, "rope", rows=True) for i in range(2)]
    seq += weave(qb[0], part[0], 1)
    seq += weave(qb[1], turns(qb[0], "qb", 0, scale=SCALE) + part[1], 2)
    moba = [dict(kind="moba", q="qb", kk="kb", v="vb", h=h, kh=h, k=8 + h) for h in range(8)]
    steps, o_moba = attention(moba)
    part = cut(steps, 4)
    part[0] = turns(qb[1], "qb", 4, scale=SCALE) + part[0]
    for i in range(4):
        seq += weave(w_in(GLA + i * CH, "gate", to="sa", off=i * CH), part[i], 3 if i == 0 else 1)
    glb = [w_in(GLB + i * CH, "gate", to="sb", off=i * CH) for i in range(4)]
    seq += weave(glb[0]) + [("load_mem", dict(after=o_moba[-1][1]))]
    seq += weave(glb[1]) + weave(glb[2], [squares(m, of="mem") for m in range(4)], 4) + weave(glb[3], [("rstd", dict(of="mem", name="mem"))])

    pend, merged = [], []
    for i in range(4):
        ya = gemm("w_dsa_o", 0, i * CH, 8, "B", 0, need=filled(o_dsa) if i == 0 else (), ev="ya", off=i * CH)
        yb = gemm("w_moba_o", 0, i * CH, 8, "B", 8, need=[(k - 8, o) for k, o in filled(o_moba)] if i == 0 else (), ev="yb", off=i * CH, rows=True)
        seq += weave(ya, pend, 3) + weave(yb)
        pend = [turn("sa", i * CH + 2 * k * P, "A", 4 * i + 2 * k, yb) for k in range(2)]
        merged += pend
    mt = [turn("mem", 2 * i * P, "B", 2 * i, rows_x, gain="g_mem_kv") for i in range(8)]
    side = [pend, mt[0:3], mt[3:6], mt[6:8]]
    wo = [gemm("w_out", 0, i * CH, KT, "A", need=filled(merged) if i == 0 else (), ev="addx", off=i * CH, rows=True)
          for i in range(4)]
    for i in range(4):
        seq += weave(wo[i], ([squares(i - 1, wo[i - 1])] if i else []) + side[i], 2 if i == 0 else 1)

    hm = [turn("x", 2 * i * P, "A", 2 * i, wo[i // 2], gain="g_mem_q") for i in range(8)]
    km = gemm("w_mem_kv", 0, 0, KT, "B", need=filled(mt), ev="plain", rstd="mem", rows=True)
    seq += weave(km, [squares(3, wo[3])] + hm, 1) + [("rstd", dict(of="x", name="h"))]
    mq = gemm("w_mem_q", 0, 0, KT, "A", need=filled(hm), ev="plain", rstd="h", rows=True)
    vm = gemm("w_mem_kv", 0, CH, KT, "B", ev="value", to="vm", off=0, rstd="mem")
    steps, o_mem = attention([dict(kind="mem", q="qm", kk="km", v="vm", h=h, kh=h, k=h) for h in range(4)])
    seq += weave(mq, turns(km, "km", 0), 3)
    seq += weave(vm, turns(mq, "qm", 0, scale=SCALE) + steps[:3] + [steps[3][:1], steps[4][:1]], 1)
    mo = [gemm("w_mem_o", 0, i * CH, 4, "B", 0, need=filled(o_mem) if i < 2 else (), ev="addx", off=i * CH, rows=True) for i in range(4)]
    (half0, half1), (half2, half3) = groups_of(mo[0]), groups_of(mo[1])
    seq += steps[3][1:] + steps[5][1:] + steps[4][1:] + steps[5][:1] + steps[6][::-1] + steps[7] + [half0, half2] + steps[8] + steps[9] + [half1, ("E", mo[0]), half3, ("E", mo[1])]
    hf = [turn("x", 2 * i * P, "A", 2 * i, mo[i // 2], gain="g_ff") for i in range(8)]
    seq += weave(mo[2], [squares(0, mo[0])] + hf[:2], 1) + weave(mo[3], [squares(1, mo[1]), squares(2, mo[2])] + hf[2:4], 1)
    pend = hf[4:6] + [squares(3, mo[3])] + hf[6:]

    def up(i, half, **more):
        return gemm("w_ff1", 0, (2 * i + half) * CH, KT, "A", ev="relu2", rstd="h", step=(0, 2 * CH), rows=True, **more)

    fa, fb = up(0, 0, need=filled(hf)), up(0, 1)
    seq += weave(fa, pend + [("rstd", dict(of="x", name="h"))], 2)
    ta = turns(fa, "B", 0)
    seq += weave(fb, ta, 3)
    segments = [(seq, 1)]
    body = []
    tb = turns(fb, "B", 4)
    fa, fb2 = up(1, 0), up(1, 1)
    body += weave(fa, tb, 3)
    down_need = filled(ta + tb)
    for m in range(4):
        body += weave(gemm("w_ff2", 0, m * CH, 8, "B", 0, need=down_need if m == 0 else (), ev="addx", off=m * CH,
                           step=(2 * CH, 0)))
    ta2 = turns(fa, "B", 0)
    body += weave(fb2, ta2, 2)
    turns_ff = FF // (2 * CH)
    segments.append((body, turns_ff - 1))

    tb = turns(fb2, "B", 4)
    seq = [("load_gain", {})]
    distances = [("distances", dict(part=i)) for i in range(8)]
    down = [gemm("w_ff2", (turns_ff - 1) * 2 * CH, m * CH, 8, "B", 0, need=filled(ta2 + tb) if m < 2 else (),
                 ev="addx", off=m * CH, rows=True) for m in range(4)]
    xt = [turn("x", 2 * i * P, "A", 2 * i, down[i // 2], gain="attn_norm_2") for i in range(8)]
    twice = [("twice", dict(m=m, rows=down[m])) for m in range(4)]
    (a0, a1, a2, a3), (b0, b1, b2, b3) = groups_of(down[0]), groups_of(down[1])
    seq += [a0, b0, tb[0], a1, tb[1], b1, distances[0], a2, distances[1], a3, ("E", down[0]), b2, distances[2], b3, ("E", down[1])]
    seq += weave(down[2], [squares(0, down[0])] + xt[:2] + [distances[3], twice[0]], 1)
    seq += weave(down[3], [squares(1, down[1]), xt[2], squares(2, down[2]), xt[3]] + distances[4:6] + [xt[4], twice[1]], 1)
    pend = [squares(3, down[3])] + [xt[5], distances[6], twice[2], xt[6], distances[7], xt[7], twice[3]]

    def w_in2(col, ev, **more):
        return gemm("w_in_2", 0, col, KT, "A", ev=ev, rstd="h", **more)

    busy = dict(rows=True, busy=True)
    qn = [w_in2(QN + i * CH, "hnorm", heads=4, **busy, need=filled(xt) if i == 0 else ()) for i in range(2)]
    kc, ks, kw = w_in2(KC, "plain", **busy), w_in2(KS, "kv", to="vs", **busy), w_in2(KW, "kv", to="vw", **busy)
    seq += weave(qn[0], pend + [("rstd", dict(of="x", name="f")), ("rstd", dict(of="x2", name="h"))], 2)
    renorm = [("renorm", dict(m=m)) for m in range(4)]
    seq += weave(kc, turns(qn[0], "qn", 0, scale=SCALE, hgain="nsa_q_norm_2"), 6)
    seq += weave(ks, [turn("stage", 0, "kc", 0, kc), turn("stage", 2 * P, "vc", 0, kc)] + renorm[:2], 3)
    blocks = [("blocks", dict(of=of, i=i)) for of in ("kc", "vc") for i in range(4)]
    seq += weave(kw, [turn("stage", 0, "ks", 0, ks, hgain="slc_k_norm_2")] + renorm[2:] + blocks[:2], 3)
    seq += weave(qn[1], [turn("stage", 0, "kw", 0, kw, hgain="win_k_norm_2")] + blocks[2:], 3)
    vf_cut = [0, VF_PART, 2 * VF_PART]
    vf = [w_in2(VF + off, "value", width=VF_PART, to="vf", off=off) for off in vf_cut[:2]]
    fg = w_in2(VF + vf_cut[2], "fg", width=FG + 32 - VF - vf_cut[2], cols2=(FG + 8 - VF - vf_cut[2], GT), off=vf_cut[2], busy=True)
    cmp = gemm(("cmp_w_k_2", "cmp_w_v_2"), 0, 0, 0, "B", 0, kind="cmp", ev="cmp", **busy)
    seq += alternate(fg, cmp)
    tq = turns(qn[1], "qn", 4, scale=SCALE, hgain="nsa_q_norm_2")
    cum = [("C", dict(which=0)), ("C", dict(which=1))]
    units = []
    for h in range(NSA_HEADS):
        kh = h // (NSA_HEADS // KV_HEADS)
        units += [dict(kind="cmp", q="qn", kk="kcmp", v="vcmp", h=h, kh=0, g=kh, b=0),
                  dict(kind="alibi", q="qn", kk="ks", v="vs", h=h, kh=kh, b=1),
                  dict(kind="alibi", q="qn", kk="kw", v="vw", h=h, kh=kh, b=2)]
    steps, o_nsa = nsa_attention(units)
    part = cut(steps, 6, NSA_SHARES)
    pend = [("gates", {})] + tq + cum + [("T", dict(src="kcmp", col=0, to="kcmp", k=0, rows=cmp, one=True))]
    for i in range(2):
        seq += weave(vf[i], pend + part[i], 2 if i == 0 else 1)
        pend = []
    for m, (name, col, i, gain, scale) in enumerate((("qf", QF, 0, "fox_q_norm_2", SCALE), ("kf", KF, 0, "fox_k_norm_2", None),
                                                     ("qf", QF, 1, "fox_q_norm_2", SCALE), ("kf", KF, 1, "fox_k_norm_2", None))):
        c = w_in2(col + i * CH, "hnorm", heads=4, rows=True)
        seq += weave(c, part[2 + m][:2] + pend + part[2 + m][2:], 4 if m else 1)
        pend = turns(c, name, 4 * i, hgain=gain, scale=scale)
    steps, o_fox = attention([dict(kind="fox", q="qf", kk="kf", v="vf", h=h, kh=h, k=h) for h in range(8)])
    part = cut(steps[:4] + pend + steps[4:], 4, (2, 5, 5, 5))
    for i in range(4):
        c = gemm("w_out_2", 1024, i * CH, 8, "B", 8, need=[(k - 8, o) for k, o in filled(o_nsa)] if i == 0 else (), ev="addx", off=i * CH)
        seq += weave(c, part[i], 4 if i == 0 else 1)
    pend, hf = [], []
    for i in range(4):
        wf = gemm("w_out_2", 0, i * CH, 8, "B", 0, need=filled(o_fox) if i == 0 else (), ev="addx", off=i * CH, rows=True)
        seq += weave(wf, pend, 3)
        pend = [turn("x", i * CH + 2 * k * P, "A", 4 * i + 2 * k, wf, gain="ffn_norm_2") for k in range(2)]
        hf += pend
        pend = [squares(i, wf)] + pend

    def gate(i, **more):
        return gemm("w_gate_2", 0, i * CH, KT, "A", ev="silu", rstd="h", step=(0, CH), **more)

    def up2(i):
        return gemm("w_up_2", 0, i * CH, KT, "A", ev="glu", rstd="h", step=(0, CH), rows=True)

    u0, u1 = up2(0), up2(1)
    seq += weave(gate(0, need=filled(hf)), pend + [("rstd", dict(of="x", name="h"))], 2) + weave(u0)
    segments.append((seq, 1))
    tg = [turn("prod", 2 * k * P, "B", 2 * k, u0) for k in range(2)]
    body = weave(gate(1), tg, 3) + weave(u1)
    for m in range(4):
        body += weave(gemm("w_down_2", 0, m * CH, 4, "B", 0, need=filled(tg) if m == 0 else (), ev="addx", off=m * CH,
                           step=(CH, 0)))
    segments.append((body, FF2 // CH - 1))
    tg = [turn("prod", 2 * k * P, "B", 2 * k, u1) for k in range(2)]
    seq, stores = list(tg), []
    for m in range(4):
        c = gemm("w_down_2", FF2 - CH, m * CH, 4, "B", 0, need=filled(tg) if m == 0 else (), ev="addx", off=m * CH, rows=True)
        seq += weave(c)
        stores.append(("store", dict(m=m, rows=c)))
    seq += stores
    segments.append((seq, 1))
    return segments


COUNTS = "gcjurs"


def number(segments):
    n = dict.fromkeys(COUNTS, 0)
    groups, landed, out = [], [0] * RING, []

    def take(what, key):
        what[key], what["ref_" + key] = n[key], n[key]
        n[key] += 1
        return what

    sums = 0
    for items, reps in segments:
        start, mine, at = dict(n), [], len(groups)
        for kind, what in items:
            if kind == "G":
                c = what["chunk"]
                if what["i"] == 0:
                    take(c, "c")
                    mine.append(c)
                take(what, "g")
                tiles = range(c["gk"] * what["i"], c["gk"] * (what["i"] + 1))
                what["need_j"] = [x["ref_j"] for k, x in c["need"] if k in tiles]
                s = what["g"] % RING
                landed[s] += 32 if c["cols2"] else 16
                groups.append(dict(chunk=c, i=what["i"], landed=landed[s], width=GROUP if c["kind"] == "cmp" else c["gk"] * c["n"]))
                c["end"] = what["g"] + 1
            elif kind in "TPOXCV":
                take(what, "j")
            elif kind == "S":
                take(what, "u")
            if kind == "E" and what["rows"]:
                if what.get("ev") not in WHOLE:
                    n["r"] += 1
                    what["r"] = what["ref_r"] = n["r"]
                if what.get("ev") in STAGED:
                    take(what, "s")
            if "rows" in what and isinstance(what["rows"], dict):
                what["rows_r"] = what["rows"].get("r_fixed", what["rows"].get("ref_r"))
                what["rows_s"] = what["rows"].get("ref_s")
                what["rows_c"] = what["rows"].get("ref_c") if what["rows"].get("ev") in WHOLE else None
            if kind == "Q":
                sums += 1
            elif kind == "rstd":
                what["sums"] = sums
            if kind == "load_mem":
                what["after_j"] = what["after"]["ref_j"]
            mine.append(what)
        per = {k: n[k] - start[k] for k in COUNTS}
        if reps > 1:
            assert per["g"] % RING == per["c"] % 2 == per["j"] % 2 == per["s"] % 2 == 0
            seen = set()
            for what in mine:
                for k in COUNTS:
                    if "ref_" + k in what and (id(what), k) not in seen:
                        seen.add((id(what), k))
                        what["ref_" + k] += per[k] * (reps - 1)
            turn_groups = groups[at:]
            for t in range(1, reps):
                groups += [dict(x, landed=x["landed"] + t * per["g"] // RING * 16) for x in turn_groups]
            landed = [x + (reps - 1) * per["g"] // RING * 16 for x in landed]
            for k in COUNTS:
                n[k] += per[k] * (reps - 1)
        out.append((items, reps, per))
    return out, groups


WHOLE = {"plain", "glu", "addx"}
STAGED = {"cq", "rope", "ropei", "idx", "plain", "hnorm", "kv", "relu2"}


class Turn:

    def __init__(self, i=0, per=None):
        per = per or dict.fromkeys(COUNTS, 0)
        self.g, self.r, self.i = i * per["g"], i * per["r"], i
        self.lo = i * (per["g"] // RING)
        self.landed = i * (per["g"] // RING * 16)
        self.c2, self.j2 = i * (per["c"] // 2), i * (per["j"] // 2)


def wait(eng, sem, n, moved=0):
    if n > 0 or not isinstance(moved, int):
        assert n > 0
        eng.wait_ge(sem, n + moved)


def two_blocks(nc, a, out):
    segments, groups = number(plan())
    ctx = ExitStack()
    with ctx:
        def sb(name, shape, dt=F32):
            return ctx.enter_context(nc.sbuf_tensor(name, shape, dt))

        def sem(name):
            return ctx.enter_context(nc.semaphore(name))

        xres = sb("xres", [P, NT, D])
        act = {"A": [sb("act_a_hi", [P, KT * SEQ], F32R), sb("act_a_lo", [P, KT * SEQ], F32R)],
               "B": [sb("act_b_hi", [P, KT * SEQ], F32R), sb("act_b_lo", [P, KT * SEQ], F32R)]}
        raw = sb("w_raw", [P, RING, GROUP])
        w_split = sb("w_split", [P, 2, RING, GROUP], F32R)
        whi, wlo = w_split[:, 0], w_split[:, 1]
        heads = sb("heads", [P, 12288])
        stage = sb("stage", [P, 2, NT, CH])
        s_sb = sb("s_sb", [P, 2, 512])
        pt_sb = sb("pt_sb", [P, 9 * P])
        scratch, act_junk = sb("scratch", [P, CH]), sb("act_junk", [P, CH])
        ident = sb("ident", [P, P])
        tri_ones = sb("tri_ones", [P, 2 * P])
        causal = sb("causal", [P, 3 * P])
        misc = sb("misc", [P, 8 * P])
        picked, score, kidx = misc[:, 0:3 * P], misc[:, 3 * P:6 * P], misc[:, 6 * P:8 * P]
        dist = misc[:, 0:3 * P]
        dist_cmp = misc[:, 3 * P:5 * P].rearrange("p (g t n) -> p g t n", g=KV_HEADS, t=NT)
        seen_cmp = misc[:, 5 * P:7 * P].rearrange("p (g t n) -> p g t n", g=KV_HEADS, t=NT)
        gains = sb("gains", [P, P])
        pos_emb = sb("pos_emb", [P, 64])
        inv = sb("inv", [P, ROPE_HALF])
        trig = sb("trig", [P, 2, NT, 2 * ROPE_HALF])
        trig8 = sb("trig8", [P, 2, NT, ROPE_HALF])
        sm = sb("small", [P, 512])
        posi = sb("posi", [P, NT], I32)
        newton_i = sb("newton_i", [P, 16], I32)
        g_rows, p_rows = stage[:, 1, 0, 0:P], stage[0:64, 1, 0, P:2 * P]
        iota_i = pt_sb[:, 0:3 * P].bitcast(I32)
        bank = [ctx.enter_context(nc.psum_tensor(f"bank{i}", [P, 512], F32)) for i in range(8)]
        prod_bank, aux_bank, s_bank = bank[0:4], bank[4:6], bank[6:8]

        at = {}

        def small(name, n):
            at[name] = (at["_end"], at["_end"] + n) if "_end" in at else (0, n)
            at["_end"] = at[name][1]
            assert at["_end"] <= 512

        for name, n in (("ss", 8), ("rstd_h", 2), ("half_h", 2), ("rstd_mem", 2), ("rstd_cq", 2), ("ss_cq", 2), ("ms", 16), ("y", 16),
                        ("t1", 16), ("hss", 16), ("hrstd", 16), ("nmax", 4), ("rsum", 4), ("rinv", 4), ("top", 8),
                        ("w_idx", 32), ("ang", 32), ("turns", 32), ("red", 32), ("sin_in", 32), ("logit", 16), ("e16", 16),
                        ("logf", 16), ("gate", 48), ("cum_q", 16), ("posf", 2), ("bias", 8), ("ss2", 8), ("rstd_f", 2), ("rm", 4)):
            small(name, n)

        def s_(name, lo=0, hi=None):
            b, e = at[name]
            return sm[:, b + lo:(e if hi is None else b + hi)]

        def part(name, off, *shape):
            n = int(np.prod(shape))
            v = heads[:, off:off + n]
            return v.rearrange("p (a b) -> p a b", a=shape[0]) if len(shape) == 2 else v

        qk = {"ka": part("ka", 0, 8, SEQ), "qa": part("qa", 2048, 8, SEQ), "kb": part("kb", 4096, 8, SEQ),
              "qb": part("qb", 6144, 8, SEQ), "qi": part("qi", 6144, 8, SEQ),
              "km": part("km", 0, 4, SEQ), "qm": part("qm", 1024, 4, SEQ),
              "qn": part("qn", 0, 8, SEQ), "kc": part("kc", 2048, 2, SEQ), "vc": part("vc", 2560, 2, SEQ),
              "ks": part("ks", 3072, 2, SEQ), "kw": part("kw", 3584, 2, SEQ), "kcmp": part("kcmp", 5120, 1, 64),
              "qf": part("qf", 6144, 8, SEQ), "kf": part("kf", 8192, 8, SEQ)}
        val = {"va": part("va", 8192, NT, 1024), "vb": part("vb", 10240, NT, 1024), "vm": part("vm", 2048, NT, CH),
               "vs": part("vs", 4096, NT, 256), "vw": part("vw", 4608, NT, 256), "vf": part("vf", 10240, NT, 1024),
               "sa": part("sa", 0, NT, D), "sb": part("sb", 4096, NT, D), "mem": part("mem", 8192, NT, D), "x": xres}
        v_cmp = heads[0:64, 5184:5312]
        k_cmp = heads[0:64, 5312:5440]
        cmp_junk = heads[0:64, 5440:5568]
        cum_t = heads[0:8, 5568:5568 + SEQ]
        gain_rows = heads[:, 6144:6144 + D]
        blk = {"kc": act["B"][0].rearrange("p (l s m) -> p l s m", l=CMP_LEN, s=2), "vc": act["B"][1].rearrange("p (l s m) -> p l s m", l=CMP_LEN, s=2)}
        rel = s_sb

        x_landed = [sem(f"x_landed{m}") for m in range(4)]
        gmix_landed, small_landed, mem_landed, gain_landed = map(sem, ("gmix_landed", "small_landed", "mem_landed", "gain_landed"))
        w_landed = [sem(f"w_landed{i}") for i in range(RING)]
        hi_ready, group_done = sem("hi_ready"), sem("group_done")
        lo_ready = [sem(f"lo_ready{i}") for i in range(RING)]
        chunk_out = [sem("chunk_out0"), sem("chunk_out1")]
        aux_done = sem("aux_done")
        aux_out = [sem("aux_out0"), sem("aux_out1")]
        rows_ready = sem("rows_ready")
        scores_done, row_max_ready, exp_done, probs_ready = map(sem, ("scores_done", "row_max_ready", "exp_done", "probs_ready"))
        squared = sem("squared")
        scored = sem("scored")
        consts_ready, alibi_ready = sem("consts_ready"), sem("alibi_ready")
        angle_ready, sine_ready = sem("angle_ready"), sem("sine_ready")
        forget_in, forget_act, gate_act = sem("forget_in"), sem("forget_act"), sem("gate_act")
        dve_step, act_step, pool_step = sem("dve_step"), sem("act_step"), sem("pool_step")
        logs_ready = sem("logs_ready")
        rstd_ready, blocks_ready = sem("rstd_ready"), sem("blocks_ready")
        stored = sem("stored")

        def pt_of(unit, slot):
            return pt_sb[:, unit["u"] % 2 * 512:unit["u"] % 2 * 512 + 512] if unit["kind"] == "mem" else pt_sb[:, slot * 3 * P:(slot + 1) * 3 * P]

        def weights(c, i, turn):
            w = a[c["w"][i // 4] if c["kind"] == "cmp" else c["w"]]
            if c["kind"] == "cmp":
                return [((0, GROUP), w[0, 8 * (i % 4):8 * (i % 4) + 8].rearrange("l d e -> d l e"), "l")]
            size = c["gk"] * P
            r, col = c["row0"] + size * i, c["col0"]
            rows, cols = slice(r, r + size), slice(col, col + c["n"])
            if not isinstance(turn.i, int):
                if c["step"][0]:
                    rows = bass.ds(turn.i * c["step"][0] + r, size)
                if c["step"][1]:
                    cols = bass.ds(turn.i * c["step"][1] + col, c["n"])
            if c["cols2"]:
                n1, col2 = c["cols2"]
                return [((0, n1), w[0, rows, col:col + n1], "c"), ((n1, c["n"]), w[0, rows, col2:col2 + c["n"] - n1], "c")]
            return [((0, c["n"]), w[0, rows, cols], "c")]

        def by_vector(g):
            return g % RING == 3 or (g % RING == 1 and not groups[g]["chunk"].get("busy"))

        def rest(engine, g):
            s, w = g % RING, groups[g]["width"]
            return engine.tensor_tensor(wlo[:, s, 0:w], raw[:, s, 0:w], whi[:, s, 0:w].bitcast(F32), ALU.subtract)

        def walk(eng, visit, name):
            for items, reps, per in segments:
                if reps == 1:
                    for kind, what in items:
                        visit(kind, what, Turn())
                else:
                    with eng.Fori(0, reps) as i:
                        turn = Turn(i, per)
                        for kind, what in items:
                            visit(kind, what, turn)

        block = ctx.enter_context(nc.Block())

        @block.sync
        def _(sp):
            def load_x(m):
                sp.dma_start(xres[:, :, m * CH:(m + 1) * CH],
                             a["x"][0, :, m * CH:(m + 1) * CH].rearrange("(t p) c -> p t c", p=P)).then_inc(x_landed[m], 16)

            vectors = []
            for name, rows in (("g_cq", 4), ("g_mem_q", KT), ("g_mem_kv", KT), ("g_ff", KT), ("attn_norm_2", KT), ("ffn_norm_2", KT),
                               ("fox_q_norm_2", 1), ("fox_k_norm_2", 1), ("nsa_q_norm_2", 1), ("cmp_k_norm_2", 1), ("slc_k_norm_2", 1),
                               ("win_k_norm_2", 1), ("g_final", KT)):
                v = a[name].rearrange("(k p) -> k p", p=P) if name == "g_final" else a[name].rearrange("a (k p) -> (a k) p", p=P)
                vectors.append((g_rows[G_ROWS[name]:G_ROWS[name] + rows, :], v))
            for i, name in enumerate(("cmp_pos_k_2", "cmp_pos_v_2")):
                vectors.append((p_rows[32 * i:32 * i + 32, :], a[name][0]))
            vectors.append((posi[:, :], a["positions"].rearrange("a (t p) -> p (a t)", p=P)))
            vectors.append((s_("bias"), a["fox_forget_bias_2"][0].partition_broadcast(P)))
            assert len(vectors) == SMALL_LOADS

            def visit(kind, what, turn):
                if kind == "G":
                    g, s = what["g"], what["g"] % RING
                    if g >= RING:
                        wait(sp, lo_ready[s], g // RING, turn.lo)
                    c = what["chunk"]
                    for (lo, hi), src, mode in weights(c, what["i"], turn):
                        if mode == "l":
                            dst = raw[:, s, :].rearrange("p (l e) -> p l e", l=8)
                        else:
                            dst = raw[:, s, 0:c["gk"] * c["n"]].rearrange("p (k n) -> p k n", k=c["gk"])[:, :, lo:hi]
                            src = src.rearrange("(k p) n -> p k n", p=P)
                        sp.dma_start(dst, src).then_inc(w_landed[s], 16)
                    if g < 4:
                        load_x(g)
                    for dst, src in vectors[3 * (g - 3):3 * (g - 2)] if g >= 3 else ():
                        sp.dma_start(dst, src, allow_slow_non_contiguous=True).then_inc(small_landed, 16)
                elif kind == "load_mem":
                    j = what["after_j"]
                    wait(sp, aux_done, j + 1)
                    for t in range(NT):
                        sp.dma_start(val["mem"][:, t, :], a["mem"][0, t * P:(t + 1) * P, :]).then_inc(mem_landed, 16)
                elif kind == "load_gain":
                    sp.dma_start(gain_rows, a["g_final"].partition_broadcast(P)).then_inc(gain_landed, 16)
                elif kind == "store":
                    m, c = what["m"], what["rows_c"]
                    wait(sp, chunk_out[c % 2], c // 2 + 1)
                    for t in range(NT):
                        sp.dma_start(out[0, t * P:(t + 1) * P, m * CH:(m + 1) * CH], xres[:, t, m * CH:(m + 1) * CH]).then_inc(stored, 16)

            walk(sp, visit, "sp")
            sp.wait_ge(stored, 16 * NT * D // CH)

        @block.gpsimd
        def _(pool):
            n = [0]

            def step(ins):
                ins.then_inc(pool_step, 1)
                n[0] += 1
                pool.wait_ge(pool_step, n[0])

            step(nc.gpsimd.memset(ident[:, :], 0.0))
            nc.gpsimd.affine_select(out=ident[:, :], in_=ident[:, :], pattern=[[-1, P]], compare_op=ALU.not_equal, fill=1.0,
                                    base=0, channel_multiplier=1).then_inc(consts_ready, 1)
            step(nc.gpsimd.memset(causal[:, :], 0.0))
            for lo in (0, 2 * P):
                step(nc.gpsimd.affine_select(out=causal[:, lo:lo + P], in_=causal[:, lo:lo + P], pattern=[[-1, P]],
                                             compare_op=ALU.is_ge, fill=NEG, base=0, channel_multiplier=1))
            step(nc.gpsimd.memset(tri_ones[:, :], 1.0))
            step(nc.gpsimd.affine_select(out=tri_ones[:, 0:P], in_=tri_ones[:, 0:P], pattern=[[1, P]],
                                         compare_op=ALU.is_ge, fill=0.0, base=0, channel_multiplier=-1))
            freq = (np.float32(THETA) ** (-np.arange(ROPE_HALF, dtype=np.float32) * np.float32(2.0 / (2 * ROPE_HALF)))).astype(np.float32)
            for i in range(ROPE_HALF):
                ins = nc.gpsimd.memset(inv[:, i:i + 1], float(freq[i]))
            ins.then_inc(consts_ready, 1)

            def distances(part):
                if part == 0:
                    step(nc.gpsimd.iota(iota_i[:, 0:P], pattern=[[-1, P]], base=0, channel_multiplier=1))
                    step(nc.gpsimd.iota(iota_i[:, P:3 * P], pattern=[[-1, 2 * P]], base=P, channel_multiplier=1))
                elif part == 1:
                    step(nc.gpsimd.tensor_copy(dist, iota_i))
                elif part == 2:
                    for lo in (0, 2 * P):
                        step(nc.gpsimd.affine_select(out=dist[:, lo:lo + P], in_=dist[:, lo:lo + P], pattern=[[-1, P]],
                                                     compare_op=ALU.is_ge, fill=FAR, base=0, channel_multiplier=1))
                elif part == 3:
                    step(nc.gpsimd.iota(iota_i[:, 0:64], pattern=[[P, NT], [-CMP_STRIDE, 32]], base=-(CMP_LEN - 1), channel_multiplier=1))
                    step(nc.gpsimd.memset(misc[:, 3 * P:5 * P], FAR))
                elif part == 4:
                    step(nc.gpsimd.memset(misc[:, 5 * P:7 * P], 0.0))
                    for g in range(KV_HEADS):
                        step(nc.gpsimd.memset(seen_cmp[:, g, :, 32 * g:32 * g + 32], 1.0))
                elif part == 5:
                    for g in range(KV_HEADS):
                        step(nc.gpsimd.tensor_copy(dist_cmp[:, g, :, 32 * g:32 * g + 32], iota_i[:, 0:64].rearrange("p (t n) -> p t n", t=NT)))
                else:
                    v, fill = ((dist_cmp, FAR), (seen_cmp, 0.0))[part - 6]
                    for g in range(KV_HEADS):
                        v_g = v[:, g, :, 32 * g:32 * g + 32]
                        ins = nc.gpsimd.affine_select(out=v_g, in_=v_g, pattern=[[P, NT], [-CMP_STRIDE, 32]], compare_op=ALU.is_ge,
                                                      fill=fill, base=-(CMP_LEN - 1), channel_multiplier=1)
                        if part == 7 and g == KV_HEADS - 1:
                            ins.then_inc(alibi_ready, 1)
                        else:
                            step(ins)

            def visit(kind, what, turn):
                if kind == "G" and not by_vector(what["g"]):
                    wait(pool, hi_ready, what["g"] + 1, turn.g)
                    rest(nc.gpsimd, what["g"]).then_inc(lo_ready[what["g"] % RING], 1)
                elif kind == "distances":
                    distances(what["part"])

            walk(pool, visit, "pool")

        @block.scalar
        def _(act_e):
            act_e.dma_start(g_rows[0:KT, :], a["g_mix"].rearrange("a (k p) -> (a k) p", p=P)).then_inc(gmix_landed, 16)
            n, rstds, xs, sums = [0], [0], [0], [0]

            def step(ins):
                ins.then_inc(act_step, 1)
                n[0] += 1
                act_e.wait_ge(act_step, n[0])

            def round_group(g, turn):
                s, w = g % RING, groups[g]["width"]
                wait(act_e, w_landed[s], groups[g]["landed"], turn.landed)
                if g >= RING:
                    wait(act_e, group_done, g - RING + 1, turn.g)
                nc.scalar.activation(whi[:, s, 0:w], raw[:, s, 0:w], ACT.Copy).then_inc(hi_ready, 1)

            for g in range(RING - 1):
                round_group(g, Turn())

            def leave(c, turn):
                ev = c["ev"]
                if ev not in ("gate", "silu"):
                    return
                wait(act_e, group_done, c["end"], turn.g)
                wait(act_e, rstd_ready, rstds[0])
                if ev == "silu" and c["c"] >= 2:
                    wait(act_e, chunk_out[(c["c"] + 1) % 2], (c["c"] + 1) // 2, turn.c2)
                for t in range(NT):
                    src = prod_bank[c["c"] % 2 * 2 + t][:, :]
                    if ev == "gate":
                        ins = nc.scalar.activation(val[c["to"]][:, t, c["off"]:c["off"] + CH], src, ACT.Tanh, scale=s_("half_h", t, t + 1))
                    else:
                        ins = nc.scalar.activation(stage[:, 0, t, :], src, ACT.Silu, scale=s_("rstd_h", t, t + 1))
                ins.then_inc(chunk_out[c["c"] % 2], 1)

            def visit(kind, what, turn):
                if kind == "G":
                    if what["g"] + RING - 1 < len(groups):
                        round_group(what["g"] + RING - 1, turn)
                elif kind == "E":
                    leave(what, turn)
                elif kind == "gates":
                    act_e.wait_ge(forget_in, 1)
                    step(nc.scalar.activation(s_("e16"), s_("e16"), ACT.Exp, scale=-1.0))
                    nc.scalar.activation(s_("e16"), s_("e16"), ACT.Ln, bias=1.0).then_inc(forget_act, 1)
                    nc.scalar.activation(s_("gate"), s_("gate"), ACT.Tanh, scale=0.5).then_inc(gate_act, 1)
                elif kind == "rope":
                    act_e.wait_ge(angle_ready, 1)
                    nc.scalar.activation(s_("sin_in"), s_("sin_in"), ACT.Sin)
                    nc.scalar.activation(s_("red"), s_("red"), ACT.Sin).then_inc(sine_ready, 1)
                elif kind == "rstd":
                    rstds[0] += 1
                elif kind == "Q":
                    m = what["m"]
                    if what["of"] == "mem":
                        act_e.wait_ge(mem_landed, 16 * NT)
                    elif "r_fixed" in what["rows"]:
                        act_e.wait_ge(x_landed[m], 16)
                    else:
                        act_e.wait_ge(chunk_out[what["rows_c"] % 2], what["rows_c"] // 2 + 1)
                    if rstds[0]:
                        act_e.wait_ge(rstd_ready, rstds[0])
                    if sums[0]:
                        act_e.wait_ge(squared, sums[0])
                    for t in range(NT):
                        ins = nc.scalar.activation(act_junk[:, :], val[what["of"]][:, t, m * CH:(m + 1) * CH], ACT.Square,
                                                   accum_out=s_("ss", 4 * t + m, 4 * t + m + 1))
                        if t == 0:
                            step(ins)
                    ins.then_inc(squared, 1)
                    sums[0] += 1
                elif kind == "X":
                    x, j = xs[0], what["j"]
                    xs[0] += 1
                    act_e.wait_ge(aux_done, j + 1)
                    if x >= 2:
                        act_e.wait_ge(scored, x - 1)
                    nc.scalar.activation(rel[:, x % 2, :], aux_bank[j % 2][:, :], ACT.Relu).then_inc(aux_out[j % 2], 1)
                elif kind == "S":
                    u = what["u"]
                    act_e.wait_ge(row_max_ready, u + 1)
                    for t, (lo, hi) in enumerate(spans(what)):
                        v = s_sb[:, u % 2, lo:hi]
                        src = s_bank[u % 2][:, lo:hi] if what["kind"] == "mem" else v
                        total = None if what["kind"] == "cmp" else s_("rsum", u % 2 * 2 + t, u % 2 * 2 + t + 1)
                        ins = nc.scalar.activation(v, src, ACT.Exp, bias=s_("nmax", u % 2 * 2 + t, u % 2 * 2 + t + 1), scale=1.0, accum_out=total)
                    ins.then_inc(exp_done, 1)

            walk(act_e, visit, "act")

        @block.tensor
        def _(pe):
            buf_j, val_c, pt_j, seen, mem_units = {}, {}, {}, set(), []

            def aux_wait(j):
                if j not in seen:
                    seen.add(j)
                    pe.wait_ge(aux_out[j % 2], j // 2 + 1)

            def group(what, turn):
                c, i, g = what["chunk"], what["i"], what["g"]
                s, par = g % RING, c["c"] % 2
                if i == 0 and c["c"] >= 2:
                    wait(pe, chunk_out[par], c["c"] // 2, turn.c2)
                for j in what["need_j"]:
                    wait(pe, aux_out[j % 2], j // 2 + 1, turn.j2)
                wait(pe, lo_ready[s], g // RING + 1, turn.lo)
                hi, lo = act[c["src"]]
                if c["kind"] == "cmp":
                    pe.wait_ge(blocks_ready, i + 1)
                    for l in range(8):
                        lhs = blk["kc" if i < 4 else "vc"][:, 8 * (i % 4) + l].rearrange("p s m -> p (s m)")
                        o = prod_bank[par * 2 + i // 4][:, 0:2 * P].rearrange("p (s e) -> p s e", s=2)
                        ins = pe.matmul(o, lhs, w_split[:, :, s, l * P:(l + 1) * P], start=i % 4 == 0 and l == 0, stop=i % 4 == 3 and l == 7)
                    ins.then_inc(group_done, 1)
                    return
                for kk in range(c["gk"]):
                    k = c["gk"] * i + kk
                    rhs_hi, rhs_lo = (w[:, s, kk * c["n"]:(kk + 1) * c["n"]] for w in (whi, wlo))
                    for t in range(NT):
                        cols = slice((c["k0"] + k) * SEQ + t * P, (c["k0"] + k) * SEQ + (t + 1) * P)
                        o = prod_bank[par * 2 + t][:, 0:c["n"]]
                        pe.matmul(o, hi[:, cols], rhs_hi, start=k == 0, stop=False)
                        pe.matmul(o, hi[:, cols], rhs_lo, start=False, stop=False)
                        ins = pe.matmul(o, lo[:, cols], rhs_hi, start=False, stop=k == c["kt"] - 1)
                ins.then_inc(group_done, 1)

            def visit(kind, what, turn):
                if kind == "init":
                    pe.wait_ge(consts_ready, 1)
                    return
                if kind == "G":
                    group(what, turn)
                    return
                if kind == "E" and what["ev"] in ("value", "kv", "cmp"):
                    val_c[what.get("to", "vcmp")] = what["c"]
                if kind == "S":
                    u = what["u"]
                    if what["q"] in buf_j:
                        aux_wait(buf_j[what["q"]])
                    aux_wait(buf_j[what["kk"]])
                    if u >= 2:
                        pe.wait_ge(row_max_ready, u - 1)
                        if mem_units and mem_units[-1] >= u - 2:
                            pe.wait_ge(exp_done, u - 1)
                    if what["kind"] == "mem":
                        mem_units.append(u)
                    q, k = qk[what["q"]][:, what["h"], :], qk[what["kk"]][:, what["kh"], :]
                    for t, (lo, hi) in enumerate(spans(what)):
                        fox = what["kind"] == "fox"
                        o = s_bank[u % 2][:, lo:hi]
                        ins = pe.matmul(o, q[:, t * P:(t + 1) * P], k[:, 0:hi - lo], start=True, stop=not fox)
                        if fox:
                            aux_wait(buf_j["cum"])
                            h = what["h"]
                            ins = pe.matmul(o, ident[0:8, h:h + 1].broadcast_to([8, P]), cum_t[:, 0:hi - lo], start=False, stop=True)
                    ins.then_inc(scores_done, 1)
                    return
                if kind not in ("T", "P", "O", "X", "C", "V"):
                    return
                j = what["j"]
                b = aux_bank[j % 2]
                if j >= 2:
                    wait(pe, aux_out[j % 2], j // 2, turn.j2)
                if kind == "V":
                    first = what["which"] == 0
                    pe.wait_ge(gmix_landed if first else small_landed, 16 if first else 16 * SMALL_LOADS)
                    rows, src = ((KT, g_rows), (N_GROWS, g_rows), (64, p_rows))[what["which"]]
                    ins = pe.transpose(b[:, 0:rows], src[0:rows, :], ident[0:rows, 0:rows])
                elif kind == "T":
                    if "r_fixed" in what["rows"]:
                        if what["src"] == "x":
                            pe.wait_ge(x_landed[what["col"] // CH], 16)
                        else:
                            pe.wait_ge(mem_landed, 16 * NT)
                    elif what["rows_c"] is not None:
                        c = what["rows_c"]
                        wait(pe, chunk_out[c % 2], c // 2 + 1, turn.c2)
                    else:
                        wait(pe, rows_ready, what["rows_r"], turn.r)
                    if what["src"] == "kcmp":
                        ins = pe.transpose(b[:, 0:64], k_cmp, ident[0:64, 0:64])
                    else:
                        src = {"stage": lambda: stage[:, what["rows_s"] % 2], "prod": lambda: stage[:, 1]}.get(what["src"], lambda: val[what["src"]])()
                        for kk in range(1 if what.get("one") else 2):
                            for t in range(NT):
                                ins = pe.transpose(b[:, kk * SEQ + t * P:kk * SEQ + (t + 1) * P],
                                                   src[:, t, what["col"] + kk * P:what["col"] + (kk + 1) * P], ident[:, :])
                    if what["to"] not in "AB":
                        buf_j[what["to"]] = j
                elif kind == "X":
                    t, w = what["t"], P * (what["t"] + 1)
                    aux_wait(buf_j["qi"])
                    aux_wait(buf_j["kidx"])
                    for i, h in enumerate(what["heads"]):
                        r = slice(64 * (h % 2), 64 * (h % 2) + 64)
                        ins = pe.matmul(b[:, i * w:(i + 1) * w], qk["qi"][r, h // 2, t * P:(t + 1) * P], kidx[r, 0:w], start=True, stop=True)
                elif kind == "P":
                    u = what["unit"]["u"]
                    pe.wait_ge(probs_ready, u + 1)
                    v = s_sb[:, u % 2, :]
                    for lo, hi, to in transposed(what["unit"]):
                        ins = pe.transpose(b[0:hi - lo, to:to + P], v[:, lo:hi], ident[:, :])
                    pt_j[u] = j
                elif kind == "O":
                    for i, (unit, slot) in enumerate(zip(what["units"], what["slots"])):
                        aux_wait(pt_j[unit["u"]])
                        cc = val_c[unit["v"]]
                        if ("c", cc) not in seen:
                            seen.add(("c", cc))
                            pe.wait_ge(chunk_out[cc % 2], cc // 2 + 1)
                        last = i == len(what["units"]) - 1
                        if unit["kind"] == "cmp":
                            ins = pe.matmul(b[:, 0:SEQ], v_cmp, pt_of(unit, slot)[0:64, 0:SEQ], start=i == 0, stop=last)
                            continue
                        v, pt = val[unit["v"]], pt_of(unit, slot)
                        h = unit["kh"] * HD
                        pe.matmul(b[:, 0:SEQ], v[:, 0, h:h + HD], pt[:, 0:SEQ], start=i == 0, stop=False)
                        o, r = (b[:, 0:SEQ], pt[:, SEQ:2 * SEQ]) if unit["kind"] == "mem" else (b[:, P:SEQ], pt[:, SEQ:3 * P])
                        ins = pe.matmul(o, v[:, 1, h:h + HD], r, start=False, stop=last)
                elif kind == "C":
                    if what["which"] == 0:
                        pe.wait_ge(logs_ready, 1)
                        pe.matmul(b[0:8, 0:SEQ], s_("logf", 0, 8), tri_ones[:, :], start=True, stop=False)
                        ins = pe.matmul(b[0:8, P:SEQ], s_("logf", 8, 16), tri_ones[:, 0:P], start=False, stop=True)
                        buf_j["cum"] = j
                    else:
                        pe.matmul(b[:, 0:8], tri_ones[:, 0:P], s_("logf", 0, 8), start=True, stop=True)
                        pe.matmul(b[:, 8:16], tri_ones[:, P:2 * P], s_("logf", 0, 8), start=True, stop=False)
                        ins = pe.matmul(b[:, 8:16], tri_ones[:, 0:P], s_("logf", 8, 16), start=False, stop=True)
                ins.then_inc(aux_done, 1)

            walk(pe, visit, "pe")

        @block.vector
        def _(dve):
            n, base, xs, taken = [0], [0], [0], set()
            v_e = nc.vector

            def step(ins):
                ins.then_inc(dve_step, 1)
                n[0] += 1
                dve.wait_ge(dve_step, base[0] + n[0])

            def rsqrt(to, ss, m, dim):
                ms, y, t1 = s_("ms", 0, m), s_("y", 0, m), s_("t1", 0, m)
                step(v_e.tensor_scalar(ms, ss, 1.0 / dim, EPS, ALU.mult, ALU.add))
                step(v_e.tensor_scalar(newton_i[:, 0:m], ms.bitcast(I32), 1, None, ALU.logical_shift_right))
                step(v_e.tensor_scalar(y.bitcast(I32), newton_i[:, 0:m], -1.0, float(0x5F3759DF), ALU.mult, ALU.add))
                for i in range(3):
                    step(v_e.tensor_tensor(t1, y, y, ALU.mult))
                    step(v_e.scalar_tensor_tensor(t1, t1, -0.5, ms, ALU.mult, ALU.mult))
                    step(v_e.scalar_tensor_tensor(to if i == 2 else y, t1, 1.5, y, ALU.add, ALU.mult))

            def rest_once(g, turn):
                if g < len(groups) and by_vector(g) and g not in taken:
                    taken.add(g)
                    wait(dve, hi_ready, g + 1, turn.g)
                    rest(v_e, g).then_inc(lo_ready[g % RING], 1)

            def early(c):
                for g in (c["end"] + 2, c["end"] + 3):
                    rest_once(g, Turn())

            def rope(v, heads, half, tr, last):
                tmp = scratch[:, 0:NT * heads * 2 * half].rearrange("p (t h d) -> p t h d", t=NT, h=heads)
                shape = [P, NT, heads, half]
                v_e.tensor_tensor(tmp[:, :, :, 0:half], v[:, :, :, half:2 * half], tr[:, 1, :, 0:half].unsqueeze(2).broadcast_to(shape), ALU.mult)
                step(v_e.tensor_tensor(tmp[:, :, :, half:], v[:, :, :, 0:half], tr[:, 1, :, half:2 * half].unsqueeze(2).broadcast_to(shape), ALU.mult))
                rot = v[:, :, :, 0:2 * half]
                step(v_e.tensor_tensor(rot, rot, tr[:, 0].unsqueeze(2).broadcast_to([P, NT, heads, 2 * half]), ALU.mult))
                ins = v_e.tensor_tensor(rot, rot, tmp, ALU.add)
                if last is None:
                    step(ins)
                else:
                    ins.then_inc(last, 1)

            def head_norm(s, heads):
                for t in range(NT):
                    sq = scratch[:, 0:heads * HD]
                    v = stage[:, s, t, 0:heads * HD]
                    step(v_e.tensor_tensor(sq, v, v, ALU.mult))
                    step(v_e.tensor_reduce(s_("hss", heads * t, heads * t + heads), sq.rearrange("p (h d) -> p h d", h=heads), AX.X, ALU.add))
                rsqrt(s_("hrstd", 0, NT * heads), s_("hss", 0, NT * heads), NT * heads, HD)
                v = stage[:, s, :, 0:heads * HD].rearrange("p t (h d) -> p t h d", h=heads)
                r = s_("hrstd", 0, NT * heads).rearrange("p (t h) -> p t h", t=NT).unsqueeze(3).broadcast_to([P, NT, heads, HD])
                v_e.tensor_tensor(v, v, r, ALU.mult).then_inc(rows_ready, 1)

            def rope_tables():
                dve.wait_ge(small_landed, 16 * SMALL_LOADS)
                dve.wait_ge(consts_ready, 2)
                step(v_e.tensor_copy(s_("posf"), posi[:, :]))
                ang, k, red, half_in = s_("ang"), s_("turns"), s_("red"), s_("sin_in")
                for t in range(NT):
                    ins = v_e.tensor_scalar(ang[:, 16 * t:16 * t + 16], inv[:, :], s_("posf", t, t + 1), None, ALU.mult)
                step(ins)
                step(v_e.tensor_scalar(k, ang, 1.0 / (2 * np.pi), MAGIC, ALU.mult, ALU.add))
                step(v_e.tensor_scalar(k, k, MAGIC, None, ALU.subtract))
                step(v_e.scalar_tensor_tensor(red, k, -TWO_PI[0], ang, ALU.mult, ALU.add))
                for part_of in TWO_PI[1:]:
                    step(v_e.scalar_tensor_tensor(red, k, -part_of, red, ALU.mult, ALU.add))
                step(v_e.tensor_scalar(red, red, PI_IN, -PI_IN, ALU.min, ALU.max))
                v_e.tensor_scalar(half_in, red, 0.5, None, ALU.mult).then_inc(angle_ready, 1)

            def rope_signs():
                dve.wait_ge(sine_ready, 1)
                sn = s_("red").rearrange("p (t i) -> p t i", t=NT)
                step(v_e.tensor_tensor(s_("ang"), s_("sin_in"), s_("sin_in"), ALU.mult))
                step(v_e.tensor_scalar(s_("ang"), s_("ang"), -2.0, 1.0, ALU.mult, ALU.add))
                cs = s_("ang").rearrange("p (t i) -> p t i", t=NT)
                for tr, half, st in ((trig, ROPE_HALF, 1), (trig8, ROPE_HALF // 2, 2)):
                    sv, cv = sn[:, :, 0:ROPE_HALF:st], cs[:, :, 0:ROPE_HALF:st]
                    v_e.tensor_copy(tr[:, 0, :, 0:half], cv)
                    v_e.tensor_copy(tr[:, 0, :, half:2 * half], cv)
                    v_e.tensor_scalar(tr[:, 1, :, 0:half], sv, -1.0, None, ALU.mult)
                    ins = v_e.tensor_copy(tr[:, 1, :, half:2 * half], sv)
                step(ins)

            def leave(c, turn):
                ev, par = c["ev"], c["c"] % 2
                out_sem, out_n = chunk_out[par], c["c"] // 2 + 1
                b = [prod_bank[par * 2 + t][:, 0:c["n"]] for t in range(NT)]
                r = [s_("rstd_" + c["rstd"], t, t + 1) for t in range(NT)] if "rstd" in c else None
                if ev == "silu":
                    return
                if ev == "gate":
                    wait(dve, out_sem, out_n)
                    v = val[c["to"]][:, :, c["off"]:c["off"] + CH]
                    step(v_e.tensor_scalar(v, v, 0.5, 0.5, ALU.mult, ALU.add))
                    return
                wait(dve, group_done, c["end"], turn.g)
                s = c["s"] % 2 if "s" in c else None

                def scaled(dst, lo, hi, final=True):
                    for t in range(NT):
                        ins = v_e.tensor_scalar(dst[t], b[t][:, lo:hi], r[t], None, ALU.mult)
                    if final:
                        ins.then_inc(out_sem, 1)

                if ev in ("cq", "rope", "ropei", "idx", "plain", "hnorm"):
                    own = c["n"]
                    if ev == "idx":
                        own = IDX_D + IDX_H
                        scaled([val["va"][:, t, c["off"]:c["off"] + c["n"] - own] for t in range(NT)], 0, c["n"] - own, final=False)
                    scaled([stage[:, s, t, 0:own] for t in range(NT)], c["n"] - own, c["n"])
                    if ev != "plain":
                        early(c)
                        wait(dve, out_sem, out_n)
                    if ev == "cq":
                        for t in range(NT):
                            v = stage[:, s, t, :]
                            ins = v_e.tensor_tensor_reduce(scratch[:, :], v, v, 1.0, 0.0, ALU.mult, ALU.add, s_("ss_cq", t, t + 1))
                            if t == 0:
                                step(ins)
                        ins.then_inc(rows_ready, 1)
                        dve.wait_ge(rows_ready, c["r"])
                        rsqrt(s_("rstd_cq"), s_("ss_cq"), NT, CH)
                    elif ev == "rope":
                        rope(stage[:, s].rearrange("p t (h d) -> p t h d", h=4), 4, ROPE_HALF, trig, rows_ready)
                    elif ev == "ropei":
                        rope(stage[:, s].rearrange("p t (h d) -> p t h d", h=8), 8, ROPE_HALF // 2, trig8, rows_ready)
                    elif ev == "idx":
                        w = s_("w_idx").rearrange("p (t h) -> p t h", t=NT)
                        step(v_e.tensor_scalar(w, stage[:, s, :, IDX_D:IDX_D + IDX_H], W_IDX_SCALE, None, ALU.mult))
                        rope(stage[:, s, :, 0:IDX_D].unsqueeze(2), 1, ROPE_HALF // 2, trig8, None)
                        v_e.tensor_copy(stage[:, s, :, IDX_D:2 * IDX_D], stage[:, s, :, 0:IDX_D]).then_inc(rows_ready, 1)
                    elif ev == "hnorm":
                        head_norm(s, c["heads"])
                elif ev == "value":
                    scaled([val[c["to"]][:, t, c["off"]:c["off"] + c["n"]] for t in range(NT)], 0, c["n"])
                elif ev == "kv":
                    scaled([stage[:, s, t, 0:2 * HD] for t in range(NT)], 0, 2 * HD, final=False)
                    scaled([val[c["to"]][:, t, :] for t in range(NT)], 2 * HD, 4 * HD)
                    early(c)
                    wait(dve, out_sem, out_n)
                    head_norm(s, 2)
                elif ev == "ya":
                    for t in range(NT):
                        g = val["sa"][:, t, c["off"]:c["off"] + CH]
                        ins = v_e.tensor_tensor(g, b[t], g, ALU.mult)
                    ins.then_inc(out_sem, 1)
                elif ev == "yb":
                    for t in range(NT):
                        g = val["sb"][:, t, c["off"]:c["off"] + CH]
                        ins = v_e.tensor_tensor(g, b[t], g, ALU.mult)
                    ins.then_inc(out_sem, 1)
                    wait(dve, out_sem, out_n)
                    ga, gb = (val[x][:, :, c["off"]:c["off"] + CH] for x in ("sa", "sb"))
                    v_e.tensor_tensor(ga, ga, gb, ALU.add).then_inc(rows_ready, 1)
                elif ev == "addx":
                    for t in range(NT):
                        x = xres[:, t, c["off"]:c["off"] + CH]
                        ins = v_e.tensor_tensor(x, b[t], x, ALU.add)
                    ins.then_inc(out_sem, 1)
                elif ev == "relu2":
                    for t in range(NT):
                        ins = v_e.tensor_scalar(stage[:, s, t, :], b[t], r[t], 0.0, ALU.mult, ALU.max)
                    ins.then_inc(out_sem, 1)
                    wait(dve, out_sem, out_n, turn.c2)
                    v_e.tensor_tensor(stage[:, s], stage[:, s], stage[:, s], ALU.mult).then_inc(rows_ready, 1)
                elif ev == "glu":
                    wait(dve, chunk_out[(c["c"] + 1) % 2], (c["c"] + 1) // 2, turn.c2)
                    for t in range(NT):
                        ins = v_e.scalar_tensor_tensor(stage[:, 1, t, :], b[t], r[t], stage[:, 0, t, :], ALU.mult, ALU.mult)
                    ins.then_inc(out_sem, 1)
                elif ev == "cmp":
                    for bb, to in zip((prod_bank[par * 2], prod_bank[par * 2 + 1]), (k_cmp, v_cmp)):
                        step(v_e.tensor_copy(cmp_junk, bb[64:128, 0:P]))
                        step(v_e.tensor_tensor(cmp_junk, bb[0:64, P:2 * P], cmp_junk, ALU.add))
                        ins = v_e.tensor_tensor(to, bb[0:64, 0:P], cmp_junk, ALU.add)
                        if to is k_cmp:
                            step(ins)
                    ins.then_inc(out_sem, 1)
                    early(c)
                    wait(dve, out_sem, out_n)
                    step(v_e.tensor_tensor_reduce(cmp_junk, k_cmp, k_cmp, 1.0, 0.0, ALU.mult, ALU.add, s_("hss", 0, 1)[0:64]))
                    rsqrt(s_("hrstd", 0, 1), s_("hss", 0, 1), 1, HD)
                    v_e.tensor_scalar(k_cmp, k_cmp, s_("hrstd", 0, 1)[0:64], None, ALU.mult).then_inc(rows_ready, 1)
                elif ev == "fg":
                    z, gt, w = s_("logit"), s_("gate"), c["n"] - 32
                    scaled([val["vf"][:, t, c["off"]:c["off"] + w] for t in range(NT)], 0, w, final=False)
                    for t in range(NT):
                        v_e.tensor_scalar(gt[:, 24 * t:24 * t + 24], b[t][:, w + 8:w + 32], r[t], None, ALU.mult)
                        ins = v_e.scalar_tensor_tensor(z[:, 8 * t:8 * t + 8], b[t][:, w:w + 8], r[t], s_("bias"), ALU.mult, ALU.add)
                    ins.then_inc(out_sem, 1)
                    wait(dve, out_sem, out_n)
                    v_e.scalar_tensor_tensor(s_("e16"), z, -1.0, z, ALU.mult, ALU.max).then_inc(forget_in, 1)

            def turned(what, turn):
                j, k = what["j"], what["k"]
                b, done = aux_bank[j % 2], aux_out[j % 2]
                if what["to"] in "AB":
                    hi, lo = act[what["to"]]
                    cols = slice(k * SEQ, (k + 2) * SEQ)
                    if "gain" not in what:
                        step(v_e.tensor_copy(hi[:, cols], b[:, :]))
                        v_e.tensor_tensor(lo[:, cols], b[:, :], hi[:, cols].bitcast(F32), ALU.subtract).then_inc(done, 1)
                        return
                    g0 = G_ROWS[what["gain"]] + (what["gain_k"] + what["col"] // P if "gain_k" in what else k)
                    for kk in range(2):
                        c1 = slice((k + kk) * SEQ, (k + kk + 1) * SEQ)
                        ins = v_e.tensor_scalar(hi[:, c1], b[:, kk * SEQ:(kk + 1) * SEQ], gains[:, g0 + kk:g0 + kk + 1], None, ALU.mult)
                    step(ins)
                    for kk in range(2):
                        c1 = slice((k + kk) * SEQ, (k + kk + 1) * SEQ)
                        ins = v_e.scalar_tensor_tensor(lo[:, c1], b[:, kk * SEQ:(kk + 1) * SEQ], gains[:, g0 + kk:g0 + kk + 1],
                                                       hi[:, c1].bitcast(F32), ALU.mult, ALU.subtract)
                    ins.then_inc(done, 1)
                    return
                scale = what.get("scale") or 1.0
                if what["src"] == "kcmp":
                    g = G_ROWS["cmp_k_norm_2"]
                    v_e.tensor_scalar(qk["kcmp"][:, 0, :], b[:, 0:64], gains[:, g:g + 1], None, ALU.mult).then_inc(done, 1)
                    return
                if what["to"] == "kidx":
                    v_e.tensor_copy(kidx, b[:, 0:SEQ]).then_inc(done, 1)
                    return
                dst = qk[what["to"]][:, k:k + 2, :]
                src = b[:, :].rearrange("p (h t) -> p h t", h=2)
                if what.get("hgain"):
                    g = G_ROWS[what["hgain"]]
                    v_e.tensor_scalar(dst, src, gains[:, g:g + 1], scale, ALU.mult, ALU.mult).then_inc(done, 1)
                else:
                    v_e.tensor_scalar(dst, src, scale, None, ALU.mult).then_inc(done, 1)

            def biased(what):
                u, kind, h = what["u"], what["kind"], what["h"]
                b, v = s_bank[u % 2], s_sb[:, u % 2, :]
                dve.wait_ge(scores_done, u + 1)
                if kind == "dsa":
                    step(v_e.tensor_tensor(v[:, 0:3 * P], b[:, 0:3 * P], picked, ALU.add))
                elif kind == "moba":
                    step(v_e.tensor_tensor(v[:, 0:3 * P], b[:, 0:3 * P], causal[:, :], ALU.add))
                elif kind == "mem":
                    v = b
                elif kind == "alibi":
                    step(v_e.scalar_tensor_tensor(v[:, 0:3 * P], dist, -SLOPES[h], b[:, 0:3 * P], ALU.mult, ALU.add))
                elif kind == "cmp":
                    d = dist_cmp[:, what["g"]].rearrange("p t n -> p (t n)")
                    step(v_e.scalar_tensor_tensor(v[:, 0:P], d, -SLOPES[h], b[:, 0:P], ALU.mult, ALU.add))
                elif kind == "fox":
                    for t, (lo, hi) in enumerate(spans(what)):
                        ins = v_e.scalar_tensor_tensor(v[:, lo:hi], b[:, lo:hi], s_("cum_q", 8 * t + h, 8 * t + h + 1), causal[:, lo:hi],
                                                       ALU.add, ALU.add)
                    step(ins)
                for t, (lo, hi) in enumerate(spans(what)):
                    i = u % 2 * 2 + t
                    ins = v_e.tensor_reduce(s_("nmax", i, i + 1), v[:, lo:hi], AX.X, ALU.max, negate=True)
                ins.then_inc(row_max_ready, 1)

            def normalised(what):
                u, i = what["u"], what["u"] % 2 * 2
                v = s_sb[:, u % 2, :]
                rs, ri = s_("rsum", i, i + 2), s_("rinv", i, i + 2)
                dve.wait_ge(exp_done, u + 1)
                if what["kind"] == "cmp":
                    for t, (lo, hi) in enumerate(spans(what)):
                        ins = v_e.tensor_tensor_reduce(v[:, lo:hi], v[:, lo:hi], seen_cmp[:, what["g"], t], 1.0, 0.0, ALU.mult, ALU.add,
                                                       s_("rsum", i + t, i + t + 1))
                    step(ins)
                    step(v_e.tensor_scalar(rs, rs, 1e-30, None, ALU.max))
                step(v_e.reciprocal(ri, rs))
                if what["kind"] in ("cmp", "alibi"):
                    g = s_("gate").rearrange("p (t x) -> p t x", t=NT)[:, :, 3 * what["h"] + what["b"]]
                    step(v_e.tensor_tensor(ri, ri, g, ALU.mult))
                for t, (lo, hi) in enumerate(spans(what)):
                    ins = v_e.tensor_scalar(v[:, lo:hi], v[:, lo:hi], s_("rinv", i + t, i + t + 1), None, ALU.mult)
                ins.then_inc(probs_ready, 1)

            def blocks(what):
                src, i = qk[what["of"]], what["i"]
                e0 = (0 if what["of"] == "kc" else CMP_LEN) + 8 * i
                to = scratch[:, :].rearrange("p (l g n) -> p l g n", l=8, g=KV_HEADS)
                step(v_e.memset(scratch[:, :], 0.0))
                half, first = 8 * i // CMP_STRIDE, 8 * i % CMP_STRIDE
                w = src[:, :, half * CMP_STRIDE:half * CMP_STRIDE + CMP_N * CMP_STRIDE].rearrange("p g (n l) -> p l g n", l=CMP_STRIDE)
                for g in range(KV_HEADS):
                    e = pos_emb[:, e0:e0 + 8].unsqueeze(2).broadcast_to([P, 8, CMP_N])
                    ins = v_e.tensor_tensor(to[:, :, g, 0:CMP_N], w[:, first:first + 8, g], e, ALU.add)
                step(ins)
                dst, from_ = blk[what["of"]][:, 8 * i:8 * i + 8], scratch[:, :].rearrange("p (l m) -> p l m", l=8)
                step(v_e.tensor_copy(dst[:, :, 0], from_))
                ins = v_e.tensor_tensor(dst[:, :, 1], from_, dst[:, :, 0].bitcast(F32), ALU.subtract)
                ins.then_inc(blocks_ready, 1)
                dve.wait_ge(blocks_ready, i + 1 if what["of"] == "kc" else i + 5)

            def visit(kind, what, turn):
                if kind == "G":
                    for g in (1, 2) if what["g"] == 0 else (what["g"] + 2,):
                        rest_once(g, turn)
                elif kind == "gates":
                    gt = s_("gate")
                    dve.wait_ge(forget_act, 1)
                    v_e.scalar_tensor_tensor(s_("logf"), s_("logit"), 0.0, s_("e16"), ALU.min, ALU.subtract).then_inc(logs_ready, 1)
                    dve.wait_ge(gate_act, 1)
                    step(v_e.tensor_scalar(gt, gt, 0.5, 0.5, ALU.mult, ALU.add))
                elif kind == "twice":
                    m = what["m"]
                    cols = slice(m * CH, (m + 1) * CH)
                    dve.wait_ge(gain_landed, 16)
                    dve.wait_ge(chunk_out[what["rows_c"] % 2], what["rows_c"] // 2 + 1)
                    for t in range(NT):
                        step(v_e.tensor_tensor(scratch[:, :], xres[:, t, cols], gain_rows[:, cols], ALU.mult))
                        step(v_e.tensor_tensor_reduce(scratch[:, :], scratch[:, :], scratch[:, :], 1.0, 0.0, ALU.mult, ALU.add,
                                                      s_("ss2", 4 * t + m, 4 * t + m + 1)))
                elif kind == "rope":
                    rope_tables()
                    rope_signs()
                elif kind == "V":
                    dve.wait_ge(aux_done, what["j"] + 1)
                    lo, hi, dst = ((0, KT, gains), (KT, N_GROWS, gains), (0, 64, pos_emb))[what["which"]]
                    v_e.tensor_copy(dst[:, lo:hi], aux_bank[what["j"] % 2][:, lo:hi]).then_inc(aux_out[what["j"] % 2], 1)
                    dve.wait_ge(aux_out[what["j"] % 2], what["j"] // 2 + 1)
                    if what["which"] == 1:
                        ga, gf = (gains[:, G_ROWS[x]:G_ROWS[x] + KT] for x in ("attn_norm_2", "g_final"))
                        step(v_e.tensor_tensor(ga, ga, gf, ALU.mult))
                elif kind == "T":
                    wait(dve, aux_done, what["j"] + 1, turn.j2 * 2)
                    turned(what, turn)
                elif kind == "P":
                    dve.wait_ge(aux_done, what["j"] + 1)
                    unit, b = what["unit"], aux_bank[what["j"] % 2]
                    m, w = {"cmp": (64, SEQ), "mem": (P, 2 * SEQ)}.get(unit["kind"], (P, 3 * P))
                    v_e.tensor_copy(pt_of(unit, what["slot"])[0:m, 0:w], b[0:m, 0:w]).then_inc(aux_out[what["j"] % 2], 1)
                elif kind == "O":
                    dve.wait_ge(aux_done, what["j"] + 1)
                    b = aux_bank[what["j"] % 2][:, 0:SEQ]
                    hi, lo = (x[:, what["k"] * SEQ:(what["k"] + 1) * SEQ] for x in act["B"])
                    step(v_e.tensor_copy(hi, b))
                    v_e.tensor_tensor(lo, b, hi.bitcast(F32), ALU.subtract).then_inc(aux_out[what["j"] % 2], 1)
                elif kind == "C":
                    dve.wait_ge(aux_done, what["j"] + 1)
                    b, done = aux_bank[what["j"] % 2], aux_out[what["j"] % 2]
                    if what["which"] == 0:
                        v_e.tensor_scalar(cum_t[:, :], b[0:8, 0:SEQ], -1.0, None, ALU.mult).then_inc(done, 1)
                    else:
                        v_e.tensor_copy(s_("cum_q"), b[:, 0:16]).then_inc(done, 1)
                        dve.wait_ge(done, what["j"] // 2 + 1)
                elif kind == "X":
                    t, x, w = what["t"], xs[0], P * (what["t"] + 1)
                    xs[0] += 1
                    dve.wait_ge(aux_out[what["j"] % 2], what["j"] // 2 + 1)
                    sc = score[:, 0:P] if t == 0 else score[:, P:3 * P]
                    for i, h in enumerate(what["heads"]):
                        r, wh = rel[:, x % 2, i * w:(i + 1) * w], s_("w_idx", 16 * t + h, 16 * t + h + 1)
                        ins = v_e.tensor_scalar(sc, r, wh, None, ALU.mult) if h == 0 else \
                            v_e.scalar_tensor_tensor(sc, r, wh, sc, ALU.mult, ALU.add)
                        if i < len(what["heads"]) - 1:
                            step(ins)
                    ins.then_inc(scored, 1)
                    dve.wait_ge(scored, x + 1)
                elif kind == "K":
                    cols = slice(0, P) if what["t"] == 0 else slice(P, 3 * P)
                    sc, top = score[:, cols], s_("top")
                    if what["part"] == 0:
                        step(v_e.tensor_tensor(sc, sc, causal[:, cols], ALU.add))
                    for _ in range(TOPK // 8 // 4):
                        step(v_e.max(top, sc))
                        step(v_e.match_replace(sc, top, sc, TAKEN))
                    if what["part"] == 3:
                        step(v_e.tensor_scalar(picked[:, cols], sc, TAKEN, NEG, ALU.not_equal, ALU.mult))
                        step(v_e.tensor_tensor(picked[:, cols], picked[:, cols], causal[:, cols], ALU.add))
                elif kind == "E":
                    leave(what, turn)
                elif kind == "rstd":
                    of, name = what["of"], what["name"]
                    dve.wait_ge(squared, what["sums"])
                    ss = s_("ss2" if of == "x2" else "ss")
                    step(v_e.tensor_reduce(s_("rm", 0, 2), ss.rearrange("p (t m) -> p t m", t=NT), AX.X, ALU.add))
                    if of == "x2":
                        for _ in range(2):
                            step(v_e.tensor_tensor(s_("rm", 0, 2), s_("rm", 0, 2), s_("rstd_f"), ALU.mult))
                    rsqrt(s_("rstd_" + name), s_("rm", 0, 2), NT, D)
                    if of == "x2":
                        step(v_e.tensor_tensor(s_("rstd_h"), s_("rstd_h"), s_("rstd_f"), ALU.mult))
                    if name == "h":
                        v_e.tensor_scalar(s_("half_h"), s_("rstd_h"), 0.5, None, ALU.mult).then_inc(rstd_ready, 1)
                    else:
                        v_e.memset(s_("t1", 0, 1), 0.0).then_inc(rstd_ready, 1)
                elif kind == "renorm":
                    m = what["m"]
                    for t in range(NT):
                        x = xres[:, t, m * CH:(m + 1) * CH]
                        ins = v_e.scalar_tensor_tensor(x, x, s_("rstd_f", t, t + 1), gain_rows[:, m * CH:(m + 1) * CH], ALU.mult, ALU.mult)
                    step(ins)
                elif kind == "blocks":
                    blocks(what)
                elif kind == "S":
                    if what["kind"] == "cmp" and what["u"] == 20:
                        dve.wait_ge(alibi_ready, 1)
                    biased(what)
                elif kind == "N":
                    normalised(what)

            for items, reps, per in segments:
                if reps == 1:
                    for kind, what in items:
                        visit(kind, what, Turn())
                else:
                    chained = sum(kind == "T" for kind, _ in items)
                    start = n[0]
                    with dve.Fori(0, reps) as i:
                        base[0] = i * chained
                        for kind, what in items:
                            visit(kind, what, Turn(i, per))
                    assert n[0] - start == chained
                    n[0] += chained * (reps - 1)
                    base[0] = 0


SMALL_LOADS = 17


def spans(unit):
    if unit["kind"] == "cmp":
        return [(0, 64), (64, 128)]
    return [(0, SEQ), (SEQ, 2 * SEQ)] if unit["kind"] == "mem" else [(0, P), (P, 3 * P)]


def transposed(unit):
    if unit["kind"] == "cmp":
        return [(0, 64, 0), (64, 128, P)]
    if unit["kind"] == "mem":
        return [(0, P, 0), (2 * P, 3 * P, P), (P, 2 * P, 2 * P), (3 * P, 4 * P, 3 * P)]
    return [(0, P, 0), (P, 2 * P, P), (2 * P, 3 * P, 2 * P)]


_INS = ["x", "mem", "positions", "g_mix", "w_in", "g_cq", "w_uq", "w_iq", "w_dsa_o", "w_moba_o", "w_out", "g_mem_q", "g_mem_kv",
        "w_mem_q", "w_mem_kv", "w_mem_o", "g_ff", "w_ff1", "w_ff2", "g_final", "attn_norm_2", "w_in_2", "fox_forget_bias_2",
        "fox_q_norm_2", "fox_k_norm_2", "nsa_q_norm_2", "cmp_k_norm_2", "slc_k_norm_2", "win_k_norm_2", "cmp_pos_k_2", "cmp_pos_v_2",
        "cmp_w_k_2", "cmp_w_v_2", "w_out_2", "ffn_norm_2", "w_gate_2", "w_up_2", "w_down_2"]


def kernel(**inputs):
    import concourse.bacc as bacc
    from concourse.bass_utils import run_bass_kernel_spmd

    nc = bacc.Bacc("TRN2", target_bir_lowering=False, num_devices=1)
    arrays, aps = {}, {}
    for name in _INS:
        v = np.ascontiguousarray(inputs[name])
        arrays["in_" + name] = v
        aps[name] = nc.dram_tensor("in_" + name, v.shape, mybir.dt.from_np(v.dtype), kind="ExternalInput").ap()
    out = nc.dram_tensor("out_y", (1, SEQ, D), F32, kind="ExternalOutput").ap()
    two_blocks(nc, aps, out)
    r = run_bass_kernel_spmd(nc, [arrays], core_ids=[0])
    return r.results[0]["out_y"]
```
